# Optimizing a Trainium2 kernel written in Bass

```python
import math
import jax, jax.numpy as jnp
from jax import lax
import numpy as np

D_MODEL = 1024
BATCH = 1
SEQ = 512
DEPTH = 2

N_A_LAYERS = DEPTH // 2
N_B_LAYERS = DEPTH - N_A_LAYERS
EPS = 1e-6

A_HEADS = 8
A_DK = 128
A_DV = 256
A_QK_W = A_HEADS * A_DK
A_V_W = A_HEADS * A_DV
A_CONV_CH = 2 * A_QK_W + A_V_W
A_IN_W = A_CONV_CH + A_V_W + 2 * A_HEADS
CONV_W = 4
CHUNK = 64

B_Q_HEADS = 32
B_KV_HEADS = 4
B_GROUP = B_Q_HEADS // B_KV_HEADS
B_HD = 64
B_W = B_Q_HEADS * B_HD
B_KV_W = B_KV_HEADS * B_HD
WINDOW = 128
BLOCK = 128

N_BUCKETS = 32
MAX_DIST = 128


def rms_norm(x, g):
    xf = x.astype(jnp.float32)
    y = xf * lax.rsqrt(jnp.mean(xf * xf, axis=-1, keepdims=True) + EPS)
    return (y * g.astype(jnp.float32)).astype(x.dtype)

def l2_norm(x):
    xf = x.astype(jnp.float32)
    return xf * lax.rsqrt(jnp.sum(xf * xf, axis=-1, keepdims=True) + EPS)

def causal_depthwise_conv(x, w):
    c = x.shape[-1]
    return lax.conv_general_dilated(
        x, w[:, None, :].astype(x.dtype), window_strides=(1,),
        padding=[(CONV_W - 1, 0)], dimension_numbers=("NWC", "WIO", "NWC"),
        feature_group_count=c)

def chunk_gated_delta_rule(q, k, v, g, beta):
    B, T, H, _ = q.shape
    N = T // CHUNK

    def chunks(t):
        return t.reshape(B, N, CHUNK, H, -1).transpose(0, 1, 3, 2, 4)

    q, k, v = chunks(q), chunks(k), chunks(v)
    g = jnp.cumsum(g.reshape(B, N, CHUNK, H).transpose(0, 1, 3, 2), axis=-1)
    beta = beta.reshape(B, N, CHUNK, H).transpose(0, 1, 3, 2)

    tri = jnp.tril(jnp.ones((CHUNK, CHUNK), dtype=bool))
    strict = jnp.tril(jnp.ones((CHUNK, CHUNK), dtype=bool), -1)
    decay = jnp.exp(jnp.where(tri, g[..., :, None] - g[..., None, :], -jnp.inf))

    kk = jnp.einsum("bnhcd,bnhsd->bnhcs", k, k)
    lower = jnp.where(strict, beta[..., :, None] * kk * decay, 0.0)
    rhs = jnp.concatenate([v * beta[..., None], k * (beta * jnp.exp(g))[..., None]], axis=-1)
    sol = lax.linalg.triangular_solve(lower, rhs, left_side=True, lower=True, unit_diagonal=True)
    u, w = sol[..., :A_DV], sol[..., A_DV:]

    qk = jnp.einsum("bnhcd,bnhsd->bnhcs", q, k) * decay
    q_dec = q * jnp.exp(g)[..., None]
    k_dec = k * jnp.exp(g[..., -1:] - g)[..., None]
    g_last = jnp.exp(g[..., -1])

    def step(S, inp):
        qk_i, qd_i, kd_i, u_i, w_i, gl_i = inp
        v_new = u_i - jnp.einsum("bhck,bhkv->bhcv", w_i, S)
        o = jnp.einsum("bhck,bhkv->bhcv", qd_i, S) + jnp.einsum("bhcs,bhsv->bhcv", qk_i, v_new)
        S = S * gl_i[..., None, None] + jnp.einsum("bhck,bhcv->bhkv", kd_i, v_new)
        return S, o

    xs = tuple(t.swapaxes(0, 1) for t in (qk, q_dec, k_dec, u, w, g_last))
    S0 = jnp.zeros((B, H, A_DK, A_DV), jnp.float32)
    _, o = lax.scan(step, S0, xs)
    return o.transpose(1, 0, 3, 2, 4).reshape(B, T, H, A_DV)

def gated_deltanet_mixer(h, w_in, conv_w, a_log, dt_bias, o_gain, w_out):
    B, T, _ = h.shape
    proj = h @ w_in
    qkv, z, ab = jnp.split(proj, [A_CONV_CH, A_CONV_CH + A_V_W], axis=-1)
    qkv = jax.nn.silu(causal_depthwise_conv(qkv, conv_w))
    q, k, v = jnp.split(qkv, [A_QK_W, 2 * A_QK_W], axis=-1)
    q = l2_norm(q.reshape(B, T, A_HEADS, A_DK)) * (A_DK ** -0.5)
    k = l2_norm(k.reshape(B, T, A_HEADS, A_DK))
    v = v.reshape(B, T, A_HEADS, A_DV).astype(jnp.float32)
    b_logit, a_logit = jnp.split(ab.astype(jnp.float32), 2, axis=-1)
    beta = jax.nn.sigmoid(b_logit)
    g = -jnp.exp(a_log.astype(jnp.float32)) * jax.nn.softplus(a_logit + dt_bias.astype(jnp.float32))
    o = chunk_gated_delta_rule(q, k, v, g, beta)
    o = rms_norm(o, o_gain) * jax.nn.silu(z.reshape(B, T, A_HEADS, A_DV).astype(jnp.float32))
    return o.reshape(B, T, A_V_W).astype(h.dtype) @ w_out

def shared_kv(x, kv_norm, w_kv, k_gain):
    B, T, _ = x.shape
    nb = T // BLOCK
    kv = rms_norm(x, kv_norm) @ w_kv
    k, v = jnp.split(kv, 2, axis=-1)
    k = rms_norm(k.reshape(B, T, B_KV_HEADS, B_HD), k_gain)
    v = v.reshape(B, T, B_KV_HEADS, B_HD)

    def band(t):
        tb = t.reshape(B, nb, BLOCK, B_KV_HEADS, B_HD)
        prev = jnp.concatenate([jnp.zeros_like(tb[:, :1]), tb[:, :-1]], axis=1)
        return jnp.concatenate([prev, tb], axis=2)

    return band(k), band(v)

def t5_causal_bucket(dist):
    n = np.maximum(dist, 0)
    max_exact = N_BUCKETS // 2
    large = max_exact + (np.log(np.maximum(n, 1) / max_exact) / np.log(MAX_DIST / max_exact)
                         * (N_BUCKETS - max_exact)).astype(np.int64)
    large = np.minimum(large, N_BUCKETS - 1)
    return np.where(n < max_exact, n, large).astype(np.int32)

def band_bias_and_mask(rel_bias, seq):
    nb = seq // BLOCK
    qi = np.arange(BLOCK)[:, None]
    s = np.arange(2 * BLOCK)[None, :]
    dist = qi + BLOCK - s
    in_window = (dist >= 0) & (dist < WINDOW)
    bias = rel_bias.astype(jnp.float32)[jnp.asarray(t5_causal_bucket(dist))]
    bias = bias.transpose(2, 0, 1).reshape(B_KV_HEADS, B_GROUP, BLOCK, 2 * BLOCK)
    key_pos = np.arange(nb)[:, None] * BLOCK - BLOCK + s
    mask = in_window[None] & (key_pos >= 0)[:, None, :]
    return bias, jnp.asarray(mask)

def swa_sink_mixer(h, w_in, q_gain, sinks, w_out, k_band, v_band, bias, mask):
    B, T, _ = h.shape
    nb = T // BLOCK
    q, z = jnp.split(h @ w_in, 2, axis=-1)
    q = rms_norm(q.reshape(B, T, B_Q_HEADS, B_HD), q_gain) * (B_HD ** -0.5)
    q = q.reshape(B, nb, BLOCK, B_KV_HEADS, B_GROUP, B_HD)
    logits = jnp.einsum("bnqkgd,bnskd->bnkgqs", q, k_band).astype(jnp.float32) + bias
    logits = jnp.where(mask[None, :, None, None], logits, -jnp.inf)
    sink = sinks.astype(jnp.float32).reshape(B_KV_HEADS, B_GROUP)[..., None, None]
    m = jnp.maximum(jnp.max(logits, axis=-1, keepdims=True), sink)
    p = jnp.exp(logits - m)
    probs = p / (jnp.sum(p, axis=-1, keepdims=True) + jnp.exp(sink - m))
    o = jnp.einsum("bnkgqs,bnskd->bnqkgd", probs.astype(v_band.dtype), v_band)
    o = o.reshape(B, T, B_W) * jax.nn.silu(z)
    return o @ w_out

def first_inputs(seed: int = 0) -> dict:
    key = jax.random.key(seed)
    ks = jax.random.split(key, 20)
    f = jnp.float32
    D = D_MODEL
    nA, nB = N_A_LAYERS, N_B_LAYERS

    def nrm(k, shape, scale):
        return jax.random.normal(k, shape, f) * scale

    dt = jnp.exp(jax.random.uniform(ks[5], (nA, A_HEADS), f, math.log(1e-3), math.log(1e-1)))
    return {
        "x": nrm(ks[0], (BATCH, SEQ, D), 1.0),
        "a_norm": 1.0 + nrm(ks[1], (nA, D), 0.02),
        "a_w_in": nrm(ks[2], (nA, D, A_IN_W), D ** -0.5),
        "a_conv": nrm(ks[3], (nA, CONV_W, A_CONV_CH), CONV_W ** -0.5),
        "a_A_log": jnp.log(jax.random.uniform(ks[4], (nA, A_HEADS), f, 1.0, 16.0)),
        "a_dt_bias": dt + jnp.log(-jnp.expm1(-dt)),
        "a_o_gain": 1.0 + nrm(ks[6], (nA, A_DV), 0.02),
        "a_w_out": nrm(ks[7], (nA, A_V_W, D), A_V_W ** -0.5),
        "kv_norm": 1.0 + nrm(ks[8], (D,), 0.02),
        "w_kv": nrm(ks[9], (D, 2 * B_KV_W), D ** -0.5),
        "k_gain": 1.0 + nrm(ks[10], (B_HD,), 0.02),
        "rel_bias": nrm(ks[11], (N_BUCKETS, B_Q_HEADS), 0.5),
        "b_norm": 1.0 + nrm(ks[12], (nB, D), 0.02),
        "b_w_in": nrm(ks[13], (nB, D, 2 * B_W), D ** -0.5),
        "b_q_gain": 1.0 + nrm(ks[14], (nB, B_HD), 0.02),
        "b_sinks": nrm(ks[15], (nB, B_Q_HEADS), 0.5),
        "b_w_out": nrm(ks[16], (nB, B_W, D), B_W ** -0.5),
    }

def first_block(x, a_norm, a_w_in, a_conv, a_A_log, a_dt_bias, a_o_gain, a_w_out,
              kv_norm, w_kv, k_gain, rel_bias,
              b_norm, b_w_in, b_q_gain, b_sinks, b_w_out):
    bias, mask = band_bias_and_mask(rel_bias, x.shape[1])
    k_band = v_band = None
    for layer in range(DEPTH):
        if layer < N_A_LAYERS:
            i = layer
            x = x + gated_deltanet_mixer(rms_norm(x, a_norm[i]), a_w_in[i], a_conv[i], a_A_log[i],
                                         a_dt_bias[i], a_o_gain[i], a_w_out[i])
            if layer == N_A_LAYERS - 1:
                k_band, v_band = shared_kv(x, kv_norm, w_kv, k_gain)
        else:
            j = layer - N_A_LAYERS
            x = x + swa_sink_mixer(rms_norm(x, b_norm[j]), b_w_in[j], b_q_gain[j], b_sinks[j],
                                   b_w_out[j], k_band, v_band, bias, mask)
    return x


DEPTH_2 = 1

POOL_WIDTH = D_MODEL // 2
POOL_WINDOWS = (2, 4, 8, 16)
N_POOL_GROUPS = len(POOL_WINDOWS)
POOL_GROUP = POOL_WIDTH // N_POOL_GROUPS
SB_WIDTH = D_MODEL - POOL_WIDTH
SB_HEAD_DIM = 64
SB_HEADS = SB_WIDTH // SB_HEAD_DIM
Q_BLOCK = 128
D_FF = 4 * D_MODEL
PLE_DIM = 256
IN_WIDTH = POOL_WIDTH + 3 * SB_WIDTH


def rms_norm_2(x, g):
    xf = x.astype(jnp.float32)
    y = xf * lax.rsqrt(jnp.mean(xf * xf, axis=-1, keepdims=True) + EPS)
    return (y * g.astype(jnp.float32)).astype(x.dtype)

def pool_mixer(u, w_pool, scale):
    b, s, _ = u.shape
    uf = u.astype(jnp.float32).reshape(b, s, N_POOL_GROUPS, POOL_GROUP)
    t = jnp.arange(s)
    outs = []
    for gi, w in enumerate(POOL_WINDOWS):
        ug = uf[:, :, gi]
        c = jnp.cumsum(ug, axis=1)
        c_prev = jnp.pad(c, ((0, 0), (w, 0), (0, 0)))[:, :s]
        cnt = jnp.minimum(t + 1, w).astype(jnp.float32)[None, :, None]
        outs.append((c - c_prev) / cnt - ug)
    d = jnp.stack(outs, axis=2).astype(u.dtype)
    y = jnp.einsum('bsgc,gcd->bsgd', d, w_pool).reshape(b, s, POOL_WIDTH)
    return y * scale

def stick_breaking_attention(q, k, v):
    b, s_len, h, dh = q.shape
    scale = dh ** -0.5
    outs = []
    for start in range(0, s_len, Q_BLOCK):
        end = start + Q_BLOCK
        qb = q[:, start:end]
        kb = k[:, :end]
        vb = v[:, :end]
        z = jnp.einsum('bqhd,bkhd->bhqk', qb, kb,
                       preferred_element_type=jnp.float32) * scale
        t_idx = start + jnp.arange(Q_BLOCK)
        s_idx = jnp.arange(end)
        mask = s_idx[None, :] < t_idx[:, None]
        log_fail = jnp.where(mask, jax.nn.log_sigmoid(-z), 0.0)
        after = lax.cumsum(log_fail, axis=3, reverse=True) - log_fail
        log_a = jax.nn.log_sigmoid(z) + after
        a = jnp.where(mask, jnp.exp(log_a), 0.0)
        outs.append(jnp.einsum('bhqk,bkhd->bqhd', a.astype(v.dtype), vb))
    return jnp.concatenate(outs, axis=1)

def second_inputs(seed: int = 0) -> dict:
    key = jax.random.key(seed)
    ks = jax.random.split(key, 20)
    f32 = jnp.float32

    def nrm(k, shape, fan_in):
        return jax.random.normal(k, shape, f32) * (fan_in ** -0.5)

    def gain(k, shape):
        return 1.0 + 0.05 * jax.random.normal(k, shape, f32)

    return {
        "x": jax.random.normal(ks[0], (BATCH, SEQ, D_MODEL), f32),
        "p": jax.random.normal(ks[1], (DEPTH_2, BATCH, SEQ, PLE_DIM), f32),
        "g_mix_pre": gain(ks[2], (DEPTH_2, D_MODEL)),
        "w_in": nrm(ks[3], (DEPTH_2, D_MODEL, IN_WIDTH), D_MODEL),
        "w_pool": nrm(ks[4], (DEPTH_2, N_POOL_GROUPS, POOL_GROUP, POOL_GROUP), POOL_GROUP),
        "pool_scale": gain(ks[5], (DEPTH_2, POOL_WIDTH)),
        "g_sb": gain(ks[6], (DEPTH_2, SB_WIDTH)),
        "w_out": nrm(ks[7], (DEPTH_2, D_MODEL, D_MODEL), D_MODEL),
        "g_mix_post": gain(ks[8], (DEPTH_2, D_MODEL)),
        "g_mlp_pre": gain(ks[9], (DEPTH_2, D_MODEL)),
        "w_up": nrm(ks[10], (DEPTH_2, D_MODEL, D_FF), D_MODEL),
        "w_down": nrm(ks[11], (DEPTH_2, D_FF, D_MODEL), D_FF),
        "g_mlp_post": gain(ks[12], (DEPTH_2, D_MODEL)),
        "w_ple_gate": nrm(ks[13], (DEPTH_2, D_MODEL, D_MODEL), D_MODEL),
        "w_ple_proj": nrm(ks[14], (DEPTH_2, PLE_DIM, D_MODEL), PLE_DIM),
        "g_ple": gain(ks[15], (DEPTH_2, D_MODEL)),
    }

def second_block(x, p, g_mix_pre, w_in, w_pool, pool_scale, g_sb, w_out, g_mix_post,
              g_mlp_pre, w_up, w_down, g_mlp_post, w_ple_gate, w_ple_proj, g_ple):
    b, s, _ = x.shape
    assert s % CHUNK == 0
    h = x
    for i in range(DEPTH_2):
        hn = rms_norm_2(h, g_mix_pre[i])
        proj = hn @ w_in[i]
        u = proj[..., :POOL_WIDTH]
        q, k, v = jnp.split(proj[..., POOL_WIDTH:], 3, axis=-1)
        q = q.reshape(b, s, SB_HEADS, SB_HEAD_DIM)
        k = k.reshape(b, s, SB_HEADS, SB_HEAD_DIM)
        v = v.reshape(b, s, SB_HEADS, SB_HEAD_DIM)

        y_pool = pool_mixer(u, w_pool[i], pool_scale[i])
        o_sb = stick_breaking_attention(q, k, v)
        y_sb = rms_norm_2(o_sb, jnp.ones((SB_HEAD_DIM,), jnp.float32)).reshape(b, s, SB_WIDTH) * g_sb[i]

        mix = jnp.concatenate([y_pool, y_sb], axis=-1) @ w_out[i]
        h = h + rms_norm_2(mix, g_mix_post[i])

        m = rms_norm_2(h, g_mlp_pre[i]) @ w_up[i]
        m = jnp.square(jax.nn.relu(m)) @ w_down[i]
        h = h + rms_norm_2(m, g_mlp_post[i])

        gate = jax.nn.sigmoid(h @ w_ple_gate[i])
        e = rms_norm_2(p[i] @ w_ple_proj[i], g_ple[i])
        h = h + gate * e
    return h


def setup_inputs(seed=0):
    out = dict(first_inputs(seed))
    for name, value in second_inputs(seed + 1).items():
        if name != "x":
            out[name + "_2"] = value
    return out


def reference(
    x, a_norm, a_w_in, a_conv, a_A_log, a_dt_bias, a_o_gain, a_w_out, kv_norm, w_kv, k_gain,
    rel_bias, b_norm, b_w_in, b_q_gain, b_sinks, b_w_out, p_2, g_mix_pre_2, w_in_2, w_pool_2,
    pool_scale_2, g_sb_2, w_out_2, g_mix_post_2, g_mlp_pre_2, w_up_2, w_down_2, g_mlp_post_2,
    w_ple_gate_2, w_ple_proj_2, g_ple_2,
):
    x = first_block(
        x, a_norm, a_w_in, a_conv, a_A_log, a_dt_bias, a_o_gain, a_w_out, kv_norm, w_kv, k_gain,
        rel_bias, b_norm, b_w_in, b_q_gain, b_sinks, b_w_out,
    )
    return second_block(
        x, p_2, g_mix_pre_2, w_in_2, w_pool_2, pool_scale_2, g_sb_2, w_out_2, g_mix_post_2,
        g_mlp_pre_2, w_up_2, w_down_2, g_mlp_post_2, w_ple_gate_2, w_ple_proj_2, g_ple_2,
    )


_drawn_inputs = setup_inputs


def setup_inputs(seed=0):
    import zlib

    import numpy as np

    out = dict(_drawn_inputs(seed))
    spreads = {}
    factors = {'a_norm': 2.865,
     'a_o_gain': 5.046,
     'kv_norm': 8.0,
     'k_gain': 8.0,
     'b_norm': 8.0,
     'b_q_gain': 8.0,
     'b_sinks': 51.439,
     'g_ple_2': 85.145,
     'g_mix_pre_2': 38.218,
     'w_pool_2': 3.931,
     'pool_scale_2': 37.643,
     'g_sb_2': 64.0,
     'g_mix_post_2': 36.258,
     'g_mlp_pre_2': 32.816,
     'w_up_2': 2.809,
     'g_mlp_post_2': 38.793}
    for name, (base, spread) in spreads.items():
        noise = np.random.default_rng([zlib.crc32(name.encode()), seed]).standard_normal(out[name].shape)
        drawn = base * np.exp(spread * noise) if base else spread * noise
        out[name] = __import__('jax').numpy.asarray(drawn.astype(out[name].dtype))
    for name, factor in factors.items():
        out[name] = (out[name] * factor).astype(out[name].dtype)
    return out
```

```python
from contextlib import ExitStack
from functools import partial

import numpy as np

import concourse.bass as bass
from concourse import mybir

F = mybir.dt.float32
R = mybir.dt.float32r
ACT = mybir.ActivationFunctionType
ALU = mybir.AluOpType
AX = mybir.AxisListType

T = 512
EPS = 1e-6
KB = 1024
SB0 = 16512

C_EPS, C_QA, C_QB, C_ONE, C_ZERO = range(5)
N_CC = 8

HEADS = 8


def block_order():
    out = []
    for i in range(HEADS + 2):
        if i >= 2:
            out += [("wa", (i - 2) * 6 + j) for j in (4, 5)]
        if i < HEADS:
            out += [("wa", i * 6 + j) for j in range(4)]
    out += [("wao", b) for b in range(16)]
    out += [("wkv", b) for b in range(4)]
    for j in range(16):
        out += [("wb", j), ("wb", 16 + j)]
    out += [("wbo", b) for b in range(16)]
    for j in range(4):
        out += [("wc", j), ("wc", 4 + j), ("wc", 8 + j)]
    out += [("wc", 12 + j) for j in range(4)]
    out += [("wco", b) for b in range(8)]
    for half in range(2):
        out += [("wu", 16 * half + b) for b in range(16)]
        out += [("wd", 16 * half + b) for b in range(16)]
    out += [("wp", b) for b in range(2)]
    out += [("wg", b) for b in range(8)]
    return out


class Op:

    __slots__ = ("eng", "fn", "deps", "used", "sem", "val")

    def __init__(self, eng, fn, deps, sem=None, val=0):
        self.eng, self.fn, self.deps, self.sem, self.val = eng, fn, deps, sem, val
        self.used = False


class Queues:

    ENGINES = ("sync", "gpsimd", "scalar", "vector", "tensor")

    def __init__(self, nc, sem):
        self.nc, self.newsem = nc, sem
        self.q = {e: [] for e in self.ENGINES}
        self.sems = {e: sem("s_" + e) for e in self.ENGINES}
        self.counts = {}

    def op(self, eng, fn, *deps):
        flat, todo = [], list(deps)
        while todo:
            x = todo.pop()
            if type(x) in (list, tuple):
                todo += x
            elif x is not None:
                flat.append(x)
        for d in flat:
            d.used = True
        o = Op(eng, fn, flat)
        self.q[eng].append(o)
        return o

    def dma(self, eng, sem, out, in_, *deps):
        if isinstance(sem, str):
            sem = self.newsem(sem)
        o = self.op(eng, lambda e: e.dma_start(out, in_), *deps)
        n = self.counts.get(sem.name, 0) + 16
        self.counts[sem.name] = n
        o.sem, o.val = sem, n
        return o

    def count(self):
        for e in self.ENGINES:
            n = 0
            for o in self.q[e]:
                if o.sem is None and o.used:
                    n += 1
                    o.val = n

    def emit(self, eng, e):
        seen = {}
        for o in self.q[eng]:
            need = {}
            for d in o.deps:
                s = d.sem if d.sem is not None else self.sems[d.eng]
                if d.val > seen.get(s.name, 0):
                    if s.name not in need or need[s.name][1] < d.val:
                        need[s.name] = (s, d.val)
            for name, (s, v) in need.items():
                e.wait_ge(s, v)
                seen[name] = v
            ins = o.fn(e)
            if o.sem is not None:
                ins.then_inc(o.sem, 16)
            elif o.used:
                ins.then_inc(self.sems[eng], 1)


class Tensor:

    def __init__(self, q):
        self.q = q

    def matmul(self, out, w, x, start, stop, after=()):
        return self.q.op("tensor", lambda e: e.matmul(out, w, x, start=start, stop=stop, skip_group_check=True),
                         *after)

    def transpose(self, out, x, ident, after=()):
        return self.q.op("tensor", lambda e: e.transpose(out, x, ident), *after)


class Vector:

    def __init__(self, q, eng="vector"):
        self.q, self.eng = q, eng

    def tensor_tensor(self, out, a, b, op, after=()):
        return self.q.op(self.eng, lambda e: e.tensor_tensor(out, a, b, op), *after)

    def tensor_scalar(self, out, a, s1, s2, op0, op1=None, after=()):
        if op1 is None:
            return self.q.op(self.eng, lambda e: e.tensor_scalar(out, a, s1, s2, op0), *after)
        return self.q.op(self.eng, lambda e: e.tensor_scalar(out, a, s1, s2, op0, op1), *after)

    def scalar_tensor_tensor(self, out, in0, scalar, in1, op0, op1, after=()):
        return self.q.op(self.eng, lambda e: e.scalar_tensor_tensor(out=out, in0=in0, scalar=scalar, in1=in1,
                                                                    op0=op0, op1=op1), *after)

    def tensor_tensor_reduce(self, out, in0, in1, scalar, op0, op1, accum_out, after=()):
        return self.q.op(self.eng, lambda e: e.tensor_tensor_reduce(out=out, in0=in0, in1=in1, scale=1.0, scalar=scalar,
                                                                    op0=op0, op1=op1, accum_out=accum_out), *after)

    def tensor_copy(self, out, a, after=()):
        return self.q.op(self.eng, lambda e: e.tensor_copy(out, a), *after)

    def reciprocal(self, out, a, after=()):
        return self.q.op(self.eng, lambda e: e.reciprocal(out, a), *after)

    def memset(self, out, v, after=()):
        return self.q.op(self.eng, lambda e: e.memset(out, v), *after)

    def affine_select(self, out, in_, compare_op, fill, base, pattern, channel_multiplier, after=()):
        return self.q.op(self.eng, lambda e: e.affine_select(out=out, in_=in_, compare_op=compare_op, fill=fill,
                                                             base=base, pattern=pattern,
                                                             channel_multiplier=channel_multiplier), *after)


class Scalar:

    def __init__(self, q):
        self.q = q

    def activation(self, out, x, func, bias=0.0, scale=1.0, accum_out=None, after=()):
        if accum_out is not None:
            return self.q.op("scalar", lambda e: e.activation(out, x, func, bias=bias, scale=scale,
                                                              accum_out=accum_out), *after)
        return self.q.op("scalar", lambda e: e.activation(out, x, func, bias=bias, scale=scale), *after)

    def preload_act_table_set(self, name):
        return self.q.op("scalar", lambda e: e.preload_act_table_set(name))


def program(nc, d, out, dump=None, stop=None):
    ctx = ExitStack()
    with ctx:
        build(nc, d, out, ctx, dump, stop)


def build(nc, d, out, ctx, dump, stop):
    def sem(n):
        return ctx.enter_context(nc.semaphore(n))

    Q = Queues(nc, sem)
    pe, ve, ac, po = Tensor(Q), Vector(Q), Scalar(Q), Vector(Q, "gpsimd")

    top = [SB0]
    names = [0]

    def at(off, shape, dt=F, name="t"):
        names[0] += 1
        return nc.alloc_sbuf_tensor_at(f"{name}{names[0]}", [128] + list(shape), dt, offset=off)

    def size(shape):
        return (int(np.prod(shape)) * 4 + 31) // 32 * 32

    def new(shape, dt=F, name="t"):
        off = top[0]
        top[0] += size(shape)
        assert top[0] <= 229344, top[0]
        return at(off, shape, dt, name)

    class Area:

        def __init__(self, lo, hi):
            self.lo, self.p, self.hi = lo, lo, hi

        def new(self, shape, dt=F, name="a"):
            off = self.p
            self.p += size(shape)
            assert self.p <= self.hi, (self.p, self.hi)
            return at(off, shape, dt, name)

    banks = [ctx.enter_context(nc.psum_tensor(f"ps{i}", [128, 512], F)) for i in range(8)]
    free = [None] * 8

    ident = new([128]); triu = new([128]); ones = new([128]); blk1 = new([128])
    ntri = new([128]); nones = new([128])
    masks = new([7, 128]); cc = new([N_CC])
    gains = new([48 + 32]); convw = new([4, 32])
    corr = new([4, 16])
    consts = Q.dma("scalar", "c0", ident[:], d["k_ident"])
    cdeps = [consts]
    for n, (t, key) in enumerate(((triu, "k_triu"), (ones, "k_ones"), (blk1, "k_blk1"), (ntri, "k_ntri"),
                                  (nones, "k_nones"), (masks, "k_masks"), (cc, "k_cc"),
                                  (convw, "a_conv"), (corr, "k_corr"))):
        cdeps.append(Q.dma("scalar", f"c{n + 1}", t[:], d[key]))
    (l_ident, l_triu, l_ones, l_blk1, l_ntri, l_nones, l_masks, l_cc, l_conv, l_corr) = cdeps
    gcol = {}
    o = 0
    gl = []
    for key, n in (("a_norm", 8), ("kv_norm", 8), ("b_norm", 8), ("g_mix_pre", 8), ("g_mix_post", 8),
                   ("g_mlp_pre", 8), ("g_mlp_post", 8), ("g_ple", 8), ("g_sb", 4), ("pool_scale", 4),
                   ("a_o_gain", 2), ("k_gain", 1), ("b_q_gain", 1)):
        gcol[key] = gains[:, o:o + n]
        gl.append(Q.dma("scalar", f"g_{key}", gains[:, o:o + n], d[key]))
        o += n
    l_gain = dict(zip(gcol, gl))

    def gain(key, i):
        return gcol[key][:, i:i + 1]

    def const(i):
        return cc[:, i:i + 1]

    NRAW, NSPL = 4, 4
    raw = new([NRAW, 1024], F, "wraw")
    wh = new([NSPL, 1024], R, "wh")
    wl = new([NSPL, 1024], R, "wl")
    order = block_order()
    rawsem = [sem(f"wr{i}") for i in range(NRAW)]
    loaded, split_lo, used = [], [], []
    AHEAD = 2

    def split(i):
        def load(j):
            key, b = order[j]
            loaded.append(Q.dma("sync", rawsem[j % NRAW], raw[:, j % NRAW, :], d[key][b],
                                split_lo[j - NRAW] if j >= NRAW else None))

        while len(loaded) < min(len(order), i + 1):
            load(len(loaded))
        r, h, lo = raw[:, i % NRAW, :], wh[:, i % NSPL, :], wl[:, i % NSPL, :]
        gone = used[i - NSPL] if i >= NSPL else None
        hi = ac.activation(h, r, ACT.Copy, after=[loaded[i], gone])
        split_lo.append(ve.tensor_tensor(lo, r, h.bitcast(F), ALU.subtract, after=[hi, gone, loaded[i]]))
        while len(loaded) < min(len(order), i + NRAW + 1):
            load(len(loaded))

    def block(key, b):
        i = len(used)
        assert order[i] == (key, b), (i, order[i], key, b)
        while len(split_lo) < min(len(order), i + 1 + AHEAD):
            split(len(split_lo))
        used.append(None)
        v = lambda w: w[:, i % NSPL, :].rearrange("p (k n) -> p k n", n=128)
        return i, v(wh), v(wl), split_lo[i]

    def mm3(bank, wa, wb, xa, xb, first, last, *deps):
        pe.matmul(bank, wa, xa, start=first, stop=False, after=[*deps])
        pe.matmul(bank, wa, xb, start=False, stop=False)
        return pe.matmul(bank, wb, xa, start=False, stop=last)

    gb_turn = [0]

    def gemm(keys, X, evac):
        for n, blocks in enumerate(keys):
            b = gb_turn[0] % 2
            gb_turn[0] += 1
            k, total = 0, 0
            for key, j in blocks:
                total += 8
            for key, j in blocks:
                i, ah, al, ready = block(key, j)
                for kk in range(8):
                    xh, xl, xr = X[k]
                    last = mm3(banks[b][:], ah[:, kk, :], al[:, kk, :], xh, xl, k == 0, k == total - 1,
                               ready if kk == 0 else None, xr, free[b] if k == 0 else None)
                    k += 1
                    if kk == 7:
                        used[i] = last
                    yield
            free[b] = evac(n, banks[b], last)
            yield

    def evac_scaled(dst, rs, post=None):
        def f(n, bank, last):
            o, dep = dst(n)
            e1 = ve.tensor_tensor(o, bank[:], rs[0][:], ALU.mult, after=[last, rs[1], dep])
            if post:
                post(n, o, e1)
            return e1
        return f

    def split_tile(src, hi, lo, *deps, scale=None):
        a = ac.activation(hi, src, ACT.Copy, after=[*deps])
        return [a, ve.tensor_tensor(lo, src, hi.bitcast(F), ALU.subtract, after=[a, *deps])]

    xreg = new([32, 512], F, "xreg")
    xoff = top[0] - 64 * KB
    XR = at(xoff, [32, 512], R, "xr")
    XF = xreg
    HOFF = top[0]
    H = new([8, 512], F, "h")
    LOC = top[0]
    END = 229344

    def rms(sq_acc, n, bank_i, tmp, rb, dep, eps_scale):
        m = pe.matmul(banks[bank_i][:], ones[:], sq_acc, start=True, stop=True, after=[dep, l_ones, free[bank_i]])
        a = ac.activation(tmp, banks[bank_i][:], ACT.Ln, bias=const(C_EPS), scale=eps_scale, after=[m, l_cc, n])
        free[bank_i] = a
        return ac.activation(rb, tmp, ACT.Exp, scale=-0.5, after=[a, n])

    tables = lambda: ac.preload_act_table_set("natural_log_exp_and_others")
    tables()

    A = Area(HOFF, END)
    GMK = 32
    x_in = [XF[:, 16 + k, :] for k in range(8)]
    ldx = [Q.dma("sync", f"x{k}", x_in[k], d["x"][k]) for k in range(8)]
    rb = A.new([512]); rtmp = A.new([512]); sqa = A.new([512]); sqt = A.new([2, 512])
    XA = []
    acc = ve.memset(sqa[:], 0.0)
    sqfree = [None, None]
    for k in range(8):
        xh, xl = XR[:, k, :], XR[:, 8 + k, :]
        s = ac.activation(sqt[:, k % 2, :], x_in[k], ACT.Square, after=[ldx[k], sqfree[k % 2]])
        acc = ve.tensor_tensor(sqa[:], sqa[:], sqt[:, k % 2, :], ALU.add, after=[s, acc])
        sqfree[k % 2] = acc
        g = gain("a_norm", k)
        hi = ac.activation(xh, x_in[k], ACT.Copy, scale=g, after=[ldx[k], l_gain["a_norm"]])
        lo = ve.scalar_tensor_tensor(
            out=xl, in0=x_in[k], scalar=g, in1=xh.bitcast(F), op0=ALU.mult, op1=ALU.subtract, after=[hi, ldx[k]])
        XA.append((xh, xl, [hi, lo]))
    rdone = rms(sqa[:], None, 2, rtmp[:], rb[:], acc, 1.0 / 1024)
    rtok = A.new([4]); rtl = A.new([4])
    m = None
    for n in range(4):
        m = pe.matmul(banks[3][:, n:n + 1], sqa[:, n * 128:(n + 1) * 128], ones[:, 0:1],
                                       start=True, stop=True, after=[acc, l_ones])
    a = ac.activation(rtl[:], banks[3][:, 0:4], ACT.Ln, bias=const(C_EPS), scale=1.0 / 1024, after=[m, l_cc])
    rtd = ac.activation(rtok[:], rtl[:], ACT.Exp, scale=-0.5, after=[a])
    free[3] = a

    woff = xoff + 31 * 2 * KB
    wab, wabh, wabl = (at(woff + 512 * n, [8, 16], t, "wab") for n, t in enumerate((F, R, R)))
    lw = Q.dma("scalar", "wab", wab[:], d["wab"])
    al = A.new([2, 8])
    lal = Q.dma("scalar", "alog", al[:], d["alog"])
    h1 = ac.activation(wabh[:], wab[:], ACT.Copy, after=[lw])
    h2 = ve.tensor_tensor(wabl[:], wab[:], wabh[:].bitcast(F), ALU.subtract, after=[h1, lw])
    for n in range(4):
        ts = slice(n * 128, (n + 1) * 128)
        for k in range(8):
            xh, xl, xr = XA[k]
            m = mm3(banks[4][:, n * 16:n * 16 + 16], xh[:, ts], xl[:, ts], wabh[:, k, :], wabl[:, k, :],
                    k == 0, k == 7, xr, h1, h2)
    ab = A.new([4, 16])
    abr = banks[4][:, 0:64].rearrange("p (n c) -> p n c", n=4)
    e0 = ve.tensor_tensor(ab[:], abr, rtok[:].unsqueeze(2).to_broadcast([128, 4, 16]), ALU.mult, after=[m, rtd])
    free[4] = e0
    sg = A.new([4, 8]); s1 = A.new([4, 8]); s2 = A.new([4, 8]); s3 = A.new([4, 8]); lnb = A.new([8, 4])
    bl, alo = ab[:, :, 0:8], ab[:, :, 8:16]
    t = ac.activation(s1[:], bl, ACT.Abs, after=[e0])
    t = ac.activation(s1[:], s1[:], ACT.Exp, scale=-1.0, after=[t])
    t = ac.activation(s1[:], s1[:], ACT.Ln, bias=const(C_ONE), after=[t])
    t_lnb = ve.scalar_tensor_tensor(out=lnb[:].rearrange("p h n -> p n h"), in0=bl, scalar=0.0, in1=s1[:],
                                                op0=ALU.min, op1=ALU.subtract, after=[t])
    t = ve.tensor_tensor(s2[:], alo, al[:, 1, :].unsqueeze(1).to_broadcast([128, 4, 8]), ALU.add, after=[lal, e0])
    t1 = ac.activation(s3[:], s2[:], ACT.Abs, after=[t])
    t1 = ac.activation(s3[:], s3[:], ACT.Exp, scale=-1.0, after=[t1])
    t1 = ac.activation(s3[:], s3[:], ACT.Ln, bias=const(C_ONE), after=[t1])
    t2 = ac.activation(al[:, 0, :], al[:, 0, :], ACT.Exp, after=[lal])
    t = ve.scalar_tensor_tensor(out=s2[:], in0=s2[:], scalar=0.0, in1=s3[:], op0=ALU.max, op1=ALU.add, after=[t1])
    gg = A.new([8, 4])
    t_g = ve.scalar_tensor_tensor(out=gg[:].rearrange("p h n -> p n h"), in0=s2[:], scalar=-1.0,
                                              in1=al[:, 0, :].unsqueeze(1).to_broadcast([128, 4, 8]),
                                              op0=ALU.mult, op1=ALU.mult, after=[t, t2])
    g32 = gg[:].rearrange("p h n -> p (h n)")
    m1 = pe.matmul(banks[2][:, 0:32], triu[:], g32, start=True, stop=True, after=[t_g, l_triu, free[2]])
    m2 = pe.matmul(banks[3][:, 0:32], ones[:], g32, start=True, stop=True, after=[t_g, free[3]])
    gcum = A.new([32]); glast = A.new([32]); gsub = A.new([32]); egn = A.new([32]); ekd = A.new([32]); egl = A.new([32])
    v1 = ve.tensor_copy(gcum[:], banks[2][:, 0:32], after=[m1])
    v2 = ve.tensor_copy(glast[:], banks[3][:, 0:32], after=[m2])
    free[2], free[3] = v1, v2
    l32 = lnb[:].rearrange("p h n -> p (h n)")
    t_gs = ve.tensor_tensor(gsub[:], gcum[:], l32, ALU.subtract, after=[v1, t_lnb])
    t = ac.activation(egn[:], gcum[:], ACT.Exp, after=[v1])
    t_egn = ve.tensor_scalar(egn[:], egn[:], -1.0, None, ALU.mult, after=[t])
    t = ve.tensor_tensor(ekd[:], glast[:], gsub[:], ALU.subtract, after=[v2, t_gs])
    t_ekd = ac.activation(ekd[:], ekd[:], ACT.Exp, after=[t])
    t_egl = ac.activation(egl[:], glast[:], ACT.Exp, after=[v2])

    cin = A.new([2, 516])
    cz = ve.memset(cin[:], 0.0)
    cfree = [cz, cz]
    qkv = A.new([2, 4, 512]); zb = A.new([2, 512])
    qkv_free = [None, None]
    z_free = [None, None]
    sqh = A.new([2, 512]); rq = A.new([2, 512])
    qd = A.new([2, 512]); qf = [None, None]
    kg = A.new([4, 128])
    kd = A.new([2, 4, 128]); vt = A.new([2, 4, 256]); wT = A.new([2, 4, 128])
    U = A.new([2, 4, 128]); qkT = A.new([2, 4, 128])
    Dm = A.new([4, 128]); AT = A.new([4, 128]); Tm = A.new([4, 128]); Pm = A.new([4, 128]); Mm = A.new([2, 4, 128])
    S = A.new([2, 256]); rr = rtmp[:].rearrange("p (a b) -> p a b", a=2); ot = sqt; osq = sqh
    state = {}
    OF = [XF[:, 16 + i, :] for i in range(16)]
    of_done = [None] * 16
    pre = {}

    later, taps = [], [0, 0]

    def conv(h, ch, j, bank, last):
        b = state.setdefault("cin", 0) % 2
        while taps[b]:
            later.pop(0)()
        state["cin"] += 1
        src, dst = cin[:, b, :], qkv[:, h % 2, j, :]
        ev = ve.tensor_tensor(src[:, 3:515], bank[:], rb[:], ALU.mult, after=[last, rdone, cfree[b]])
        t = ac.activation(dst, src[:, 3:515], ACT.Copy, scale=convw[:, 3, ch:ch + 1], after=[ev, l_conv, qkv_free[h % 2]])
        cfree[b] = t
        mine = pre.setdefault(h, [None] * 4)
        mine[j] = t

        def tap(w):
            cfree[b] = mine[j] = ve.scalar_tensor_tensor(out=dst, in0=src[:, w:w + 512], scalar=convw[:, w, ch:ch + 1],
                                                         in1=dst, op0=ALU.mult, op1=ALU.add,
                                                         after=[mine[j], ev, l_conv])
            taps[b] -= 1

        taps[b] = 3
        for w in range(3):
            later.append(partial(tap, w))
        return ev

    def gemm_head(h):
        yield from gemm([[("wa", 6 * h + j)] for j in range(4)], XA,
                        lambda n, bank, last: conv(h, [h, 8 + h, 16 + 2 * h, 17 + 2 * h][n], n, bank, last))

    def gemm_z(h):
        zs = []

        def ev(n, bank, last):
            e1 = ve.tensor_tensor(zb[:, n, :], bank[:], rb[:], ALU.mult, after=[last, rdone, z_free[n]])
            zs.append(e1)
            return e1

        yield from gemm([[("wa", 6 * h + 4 + j)] for j in range(2)], XA, ev)
        state[("z", h)] = zs

    def bk(i):
        return banks[i][:].rearrange("p (n c) -> p n c", n=4)

    turn = [0]

    def xbank():
        turn[0] += 1
        return 2 + turn[0] % 2

    def bc(v, w=128):
        return v.unsqueeze(2).to_broadcast([128, 4, w])

    def prep(h):
        p = h % 2
        col = slice(4 * h, 4 * h + 4)
        b = xbank()
        for n in range(4):
            m = pe.matmul(bk(b)[:, n, :], gg[:, h, n:n + 1].to_broadcast([128, 128]), triu[:],
                                                start=True, stop=True, after=[free[b] if n == 0 else None, t_g, l_triu])
        yield
        dv = ve.tensor_tensor(Dm[:], bk(b), bc(gsub[:, col]), ALU.subtract, after=[m, t_gs, state.get("Dfree")])
        egb = rq[:, 1, :]
        sel = po.affine_select(out=Dm[:], in_=Dm[:], compare_op=ALU.is_ge, fill=-1.0e4, base=0,
                               pattern=[[0, 4], [1, 128]], channel_multiplier=-1, after=[dv])
        silus, sqs = [], []
        for j in range(2):
            v = qkv[:, p, j, :]
            silus.append(ac.activation(v, v, ACT.Silu, after=[pre[h][j]]))
        for j in range(2):
            sqs.append(ac.activation(sqh[:, j, :], qkv[:, p, j, :], ACT.Square,
                                     after=[silus[j], state.get(("sqh", j))]))
        for j in range(2, 4):
            v = qkv[:, p, j, :]
            silus.append(ac.activation(v, v, ACT.Silu, after=[pre[h][j]]))
        tables()
        yield
        yield
        yield
        q, k = qkv[:, p, 0, :], qkv[:, p, 1, :]
        norm, sums = [], []
        for j in range(2):
            c = xbank()
            m = pe.matmul(banks[c][:], ones[:], sqh[:, j, :], start=True, stop=True, after=[sqs[j], free[c]])
            state[("sqh", j)] = m
            sums.append((c, m))
            if j == 0:
                eb = ac.activation(egb, banks[b][:], ACT.Exp, after=[dv, state.get("rqfree")])
                free[b] = [dv, eb]
                yield
        for j, v in enumerate((q, k)):
            c, m = sums[j]
            l = ac.activation(rq[:, 0, :], banks[c][:], ACT.Ln, bias=const(C_EPS), after=[m, state.get("rq0"), l_cc])
            free[c] = l
            x = ac.activation(rq[:, 0, :], rq[:, 0, :], ACT.Exp, scale=-0.5,
                              bias=const(C_QA) if j == 0 else const(C_ZERO), after=[l])
            y = ve.tensor_tensor(v, v, rq[:, 0, :], ALU.mult, after=[x, silus[j]])
            state["rq0"] = y
            norm.append(y)
            yield
            yield
        E = ac.activation(Dm[:], Dm[:], ACT.Exp, after=[sel])
        qdn = ve.tensor_tensor(qd[:, p, :], q, egb, ALU.mult, after=[norm[0], eb, qf[p]])
        state["rqfree"] = qdn
        b = xbank()
        ch = [slice(n * 128, (n + 1) * 128) for n in range(4)]
        for n in range(4):
            m = pe.matmul(bk(b)[:, n, :], k[:, ch[n]], k[:, ch[n]], start=True, stop=True, after=[norm[1], free[b] if n == 0 else None])
        at_ = ve.tensor_tensor(AT[:], bk(b), Dm[:], ALU.mult, after=[m, E, state.get("ATfree")])
        free[b] = at_
        yield
        b = xbank()
        for n in range(4):
            m = pe.matmul(bk(b)[:, n, :], k[:, ch[n]], q[:, ch[n]], start=True, stop=True, after=[norm, free[b] if n == 0 else None])
        qk = ve.tensor_tensor(qkT[:, p], bk(b), Dm[:], ALU.mult, after=[m, E, state.get(("rec", p))])
        free[b] = qk
        state["Dfree"] = qk
        yield
        b = xbank()
        for n in range(4):
            m = pe.transpose(bk(b)[:, n, :], k[:, ch[n]], ident[:], after=[norm[1], l_ident, free[b] if n == 0 else None])
        kgo = ve.tensor_tensor(kg[:], bk(b), bc(egn[:, col]), ALU.mult, after=[m, t_egn, state.get("kgfree")])
        kdo = ve.tensor_tensor(kd[:, p], bk(b), bc(ekd[:, col]), ALU.mult, after=[m, t_ekd, state.get(("rec", p))])
        free[b] = [kgo, kdo]
        state[("kdo", h)] = kdo
        yield
        vts = []
        for j in range(2):
            b = xbank()
            v = qkv[:, p, 2 + j, :]
            for n in range(4):
                m = pe.transpose(bk(b)[:, n, :], v[:, ch[n]], ident[:], after=[silus[2 + j], free[b] if n == 0 else None])
            c = ac.activation(vt[:, p, :, j * 128:(j + 1) * 128], bk(b), ACT.Copy, after=[m, state.get(("rec", p))])
            free[b] = c
            vts.append(c)
            yield
        qkv_free[p] = [qdn, m]
        def level(i, dep):
            s = Mm[:, i % 2]
            return po.tensor_tensor(s, AT[:], masks[:, i, :].unsqueeze(1).to_broadcast([128, 4, 128]),
                                                ALU.mult, after=[dep, l_masks])
        mk = level(0, [at_, state.get("Mfree1")])
        mn = level(1, [at_, state.get("Mfree2")])
        Up = U[:, p]
        u = ve.tensor_tensor(Up, ident[:].unsqueeze(1).to_broadcast([128, 4, 128]), Mm[:, 0],
                                         ALU.subtract, after=[mk, l_ident, state.get(("rec", p))])
        b = xbank()
        for n in range(4):
            m = pe.transpose(bk(b)[:, n, :], Up[:, n, :], ident[:], after=[u, free[b] if n == 0 else None])
        t = ac.activation(Tm[:], bk(b), ACT.Copy, after=[m, state.get("Tfree")])
        free[b] = t
        yield
        u0 = u
        for i in range(1, 7):
            b = xbank()
            s = Mm[:, i % 2]
            for n in range(4):
                m = pe.matmul(bk(b)[:, n, :], s[:, n, :], Tm[:, n, :], start=True, stop=True,
                              after=[t, mn, free[b] if n == 0 else None])
            state["Tfree"] = m
            pc = ac.activation(Pm[:], bk(b), ACT.Copy, after=[m, state.get("Pfree")])
            free[b] = pc
            if i < 6:
                mn = level(i + 1, [u0 if i == 1 else prev])
                if i == 5:
                    state["ATfree"] = mn
            else:
                state["Mfree2"] = m
            prev = m
            if i == 6:
                state["Mfree1"] = m
            yield
            mt = None
            if i < 6:
                b = xbank()
                for n in range(4):
                    mt = pe.matmul(bk(b)[:, n, :], Up[:, n, :], Pm[:, n, :], start=True, stop=True,
                                   after=[pc, u, free[b] if n == 0 else None])
                t = ve.tensor_tensor(Tm[:], Tm[:], bk(b), ALU.subtract, after=[mt, t])
                free[b] = t
            b = xbank()
            for n in range(4):
                m = pe.matmul(bk(b)[:, n, :], Pm[:, n, :], Up[:, n, :], start=True, stop=True,
                              after=[pc, u, free[b] if n == 0 else None])
            state["Pfree"] = m
            u = ve.tensor_tensor(Up, Up, bk(b), ALU.subtract, after=[m, u])
            free[b] = u
            yield
        b = xbank()
        for n in range(4):
            m = pe.matmul(bk(b)[:, n, :], kg[:, n, :], Up[:, n, :], start=True, stop=True, after=[u, kgo, free[b] if n == 0 else None])
        state["kgfree"] = m
        w = ac.activation(wT[:, p], bk(b), ACT.Copy, after=[m, state.get(("rec", p))])
        free[b] = w
        state[("rdy", h)] = [u, w, qk, kdo, qdn] + vts
        yield

    def recur(h):
        p = h % 2
        rdy = state[("rdy", h)]
        s = None
        for n in range(4):
            Sn, So = S[:, (n + 1) % 2], S[:, n % 2]
            ts = slice(n * 128, (n + 1) * 128)
            m = pe.matmul(banks[4][:, 0:256], U[:, p, n, :], vt[:, p, n, :], start=True, stop=(n == 0), after=[rdy, free[4]])
            if n:
                m = pe.matmul(banks[4][:, 0:256], wT[:, p, n, :], So, start=False, stop=True, after=[s])
            rn = rr[:, n % 2]
            r = ac.activation(rn, banks[4][:, 0:256], ACT.Copy, after=[m, state.get(("rr", n % 2))])
            free[4] = r
            yield
            if n < 3:
                m = pe.matmul(banks[5][:, 0:256], kd[:, p, n, :], rn, start=True, stop=True, after=[r, free[5]])
                if n == 0:
                    s2_ = ve.tensor_copy(Sn, banks[5][:, 0:256], after=[m, state.get("Sfree")])
                else:
                    s2_ = ve.scalar_tensor_tensor(
                        out=Sn, in0=So, scalar=egl[:, 4 * h + n:4 * h + n + 1], in1=banks[5][:, 0:256],
                        op0=ALU.mult, op1=ALU.add, after=[m, t_egl, state.get("Sfree"), s])
                free[5] = s2_
            for j in range(2):
                o_ = banks[6 + j][:, ts]
                dj = slice(j * 128, (j + 1) * 128)
                if n:
                    pe.matmul(o_, So[:, dj], qd[:, p, ts], start=True, stop=False, after=[s, free[6 + j]])
                m = pe.matmul(o_, rn[:, dj], qkT[:, p, n, :], start=(n == 0), stop=True, after=[r, free[6 + j] if n == 0 else None])
            state[("rr", n % 2)] = m
            state["Sfree"] = m
            s = s2_
            yield
        state[("rec", p)] = m
        qf[p] = m
        sq, tt = [], []
        for j in range(2):
            sq.append(ac.activation(osq[:, j, :], banks[6 + j][:], ACT.Square, after=[m, state.get(("sqh", j))]))
        yield
        for j in range(2):
            mo = pe.matmul(banks[5][:], ones[:], osq[:, j, :], start=(j == 0), stop=(j == 1), after=[sq[j], free[5]])
        state[("sqh", 1)] = mo
        zs = []
        for j in range(2):
            z = zb[:, j, :]
            zs.append(ac.activation(z, z, ACT.Silu, after=[state[("z", h)][j]]))
        tables()
        for j in range(2):
            x = ve.scalar_tensor_tensor(out=ot[:, j, :], in0=banks[6 + j][:],
                                                         scalar=gain("a_o_gain", j), in1=zb[:, j, :],
                                                         op0=ALU.mult, op1=ALU.mult, after=[sq[j], zs[j], l_gain["a_o_gain"], state.get(("ot", j))])
            free[6 + j] = [sq[j], x]
            z_free[j] = x
            tt.append(x)
        l = ac.activation(osq[:, 0, :], banks[5][:], ACT.Ln, bias=const(C_EPS), scale=1.0 / 256, after=[mo])
        free[5] = l
        l = ac.activation(osq[:, 0, :], osq[:, 0, :], ACT.Exp, scale=-0.5, after=[l])
        for j in range(2):
            w = ve.tensor_tensor(OF[2 * h + j], ot[:, j, :], osq[:, 0, :], ALU.mult, after=[l, tt[j], xin_free])
            state[("ot", j)] = w
            of_done[2 * h + j] = w
        state[("sqh", 0)] = w
        yield

    xin_free = [x for _, _, r in XA for x in r] + [acc]

    OH = [(XR[:, i, :], XR[:, 16 + i, :]) for i in range(16)]
    XO = [None] * 16

    def split_o(lo, hi):
        for i in range(lo, hi):
            XO[i] = (*OH[i], split_tile(OF[i], *OH[i], of_done[i], used[-1]))
            yield

    fill = {HEADS: 0.7, HEADS + 1: 4}
    for i in range(HEADS + 2):
        gen = [gemm_z(i - 2)] if i >= 2 else []
        gen += [gemm_head(i)] if i < HEADS else []
        gen += [split_o(0, 14)] if i == HEADS + 1 else []
        merge(chain(*gen), fill.get(i, 1.45), prep(i - 1) if 1 <= i <= HEADS else None, spread(recur(i - 2), 2) if i >= 2 else None,
              later=later)
    drain(split_o(14, 16))

    if stop == "A":
        dumps = [dump(Q, f"OF{i}", OF[i], of_done[i]) for i in range(16)]
        return finish(Q, ctx, loaded[-4:] + dumps)

    sqt = new([2, 512]); sqa = new([512]); rb = new([512]); rt = new([512])
    LOC = top[0]
    a_done = [of_done[15], used[-1], x_last(Q, "scalar"), x_last(Q, "tensor"), x_last(Q, "gpsimd")]
    ldh = [Q.dma("scalar", f"xr{k}", H[:, k, :], d["x"][k], a_done) for k in range(8)]
    norm = {}

    def stats(n, tile, dep):
        s = ac.activation(sqt[:, n % 2, :], tile, ACT.Square, after=[dep, norm.get(n % 2)])
        if n == 0:
            a = ve.tensor_copy(sqa[:], sqt[:, 0, :], after=[s, norm.get("acc")])
        else:
            a = ve.tensor_tensor(sqa[:], sqa[:], sqt[:, n % 2, :], ALU.add, after=[s, norm["acc"]])
        norm[n % 2] = norm["acc"] = a
        return a

    def rstd():
        m = pe.matmul(banks[2][:], ones[:], sqa[:], start=True, stop=True, after=[norm["acc"], l_ones, free[2]])
        a = ac.activation(rt[:], banks[2][:], ACT.Ln, bias=const(C_EPS), scale=1.0 / 1024, after=[m, l_cc])
        free[2] = a
        norm["acc"] = m
        return ac.activation(rb[:], rt[:], ACT.Exp, scale=-0.5, after=[a, norm.get("rb")])

    def scaled_split(key, dst, ready, *deps):
        X = []
        for k in range(8):
            xh, xl = dst[k]
            g = gain(key, k)
            hi = ac.activation(xh, H[:, k, :], ACT.Copy, scale=g, after=[ready[k], l_gain[key], deps])
            lo = ve.scalar_tensor_tensor(out=xl, in0=H[:, k, :], scalar=g, in1=xh.bitcast(F),
                                         op0=ALU.mult, op1=ALU.subtract, after=[hi, ready[k], deps])
            X.append((xh, xl, [hi, lo]))
        return X

    h_ready = [None] * 8

    def evac_h(dep):
        def f(n, bank, last):
            h_ready[n] = ve.tensor_tensor(H[:, n, :], bank[:], H[:, n, :], ALU.add, after=[last, dep[n]])
            stats(n, H[:, n, :], h_ready[n])
            return h_ready[n]
        return f

    norm["acc"] = norm[0] = norm[1] = a_done
    drain(gemm([[("wao", 2 * n), ("wao", 2 * n + 1)] for n in range(8)], XO, evac_h(ldh)))
    if stop == "x1":
        dumps = [dump(Q, f"H{i}", H[:, i, :], h_ready[i]) for i in range(8)]
        return finish(Q, ctx, loaded[-4:] + dumps)

    def slot(i):
        return XR[:, i, :]

    B = Area(LOC, END)
    kpad = B.new([4, 2, 512]); vz = B.new([4, 9, 64])
    qb = B.new([3, 512]); bias = B.new([2, 2, 256]); L = B.new([2, 2, 4, 256]); pT = B.new([4, 4, 128])
    sinks = B.new([32]); mx = B.new([2, 8]); nmx = B.new([2, 8]); den = B.new([2, 8]); es = B.new([2, 8])
    rel = B.new([32]); flip = B.new([128]); hot = L[:, 0].rearrange("p a b c -> p (a b c)")[:, 0:384]
    neg = L[:, 0].rearrange("p a b c -> p (a b c)")[:, 512:896]
    tab = L[:, 0].rearrange("p a b c -> p (a b c)")[:, 1024:1408]
    kst = L[:, 1].rearrange("p a b c -> p (a b c)")[:, 0:1024].rearrange("p (a b) -> p a b", a=2)
    scratch = nc.dram_tensor("rel_rows", [32 * 384], F, kind="Internal").ap()
    w_done = used[-1]
    l_flip = Q.dma("scalar", "flip", flip[:], d["k_flip"], a_done)
    l_rel = Q.dma("scalar", "rel", rel[0:32, :], d["rel"], a_done)
    l_hot = Q.dma("scalar", "hot", hot[0:32, :], d["k_hot"], a_done)
    l_neg = Q.dma("scalar", "neg", neg[0:32, :], d["k_neg"], a_done)
    l_snk = Q.dma("scalar", "snk", sinks[:], d["sinks"], a_done)
    z1 = po.memset(kpad[:], 0.0, after=a_done)
    z2 = po.memset(vz[:], 0.0, after=a_done)

    m = pe.matmul(banks[3][0:32, 0:384], rel[0:32, :], hot[0:32, :], start=True, stop=True,
                  after=[l_rel, l_hot, free[3]])
    t = ve.tensor_tensor(tab[0:32, :], banks[3][0:32, 0:384], neg[0:32, :], ALU.add, after=[m, l_neg, a_done])
    free[3] = t
    tab_out = Q.dma("scalar", "tabo", scratch.rearrange("(h j) -> h j", h=32), tab[0:32, :], t)

    XKV = scaled_split("kv_norm", [(slot(16 + k), slot(24 + k)) for k in range(8)], h_ready, w_done)
    XB = scaled_split("b_norm", [(slot(k), slot(8 + k)) for k in range(8)], h_ready, w_done)
    r1 = rstd()
    vtiles = []

    def head_rms(x, ops, n, tmp, sq, key, dep):
        s = ac.activation(sq, x, ACT.Square, after=[ops, dep])
        b = xbank()
        m = pe.matmul(banks[b][:], blk1[:], sq, start=True, stop=True, after=[s, l_blk1, free[b]])
        a = ac.activation(tmp, banks[b][:], ACT.Ln, bias=const(C_EPS), scale=1.0 / 64, after=[m, dep])
        free[b] = a
        a = ac.activation(tmp, tmp, ACT.Exp, scale=-0.5, bias=const(n), after=[a])
        return ve.scalar_tensor_tensor(out=x, in0=x, scalar=gain(key, 0), in1=tmp, op0=ALU.mult, op1=ALU.mult,
                                       after=[a, l_gain[key]])

    kq = {}

    def evac_kv(n, bank, last):
        if n < 2:
            dst = kst[:, n, :]
        else:
            dst = qb[:, n - 2, :]
        e1 = ve.tensor_tensor(dst, bank[:], rb[:], ALU.mult, after=[last, r1, a_done])
        kq[n] = e1
        return e1

    kn = {}
    copies = {}

    def kv_post():
        for n in range(2):
            sq = pT[:].rearrange("p a b c -> p (a b c)")[:, 512 * n:512 * n + 512]
            tm = pT[:].rearrange("p a b c -> p (a b c)")[:, 1024 + 512 * n:1536 + 512 * n]
            kn[n] = head_rms(kst[:, n, :], kq[n], C_ZERO, tm, sq, "k_gain", a_done)
            for hh in range(2):
                g = 2 * n + hh
                src = kst[64 * hh:64 * hh + 64, n, :]
                copies[g] = [Q.dma("sync", f"kp{g}{e}", kpad[64 * e:64 * e + 64, g, e, :], src, kn[n], z1)
                             for e in range(2)]
        for n in range(2):
            b = xbank()
            for c in range(4):
                m = pe.transpose(bk(b)[:, c, :], qb[:, n, c * 128:(c + 1) * 128], ident[:],
                                 after=[kq[2 + n], l_ident, free[b]])
            for hh in range(2):
                g = 2 * n + hh
                t = ac.activation(vz[:, :, 2 * g + 1, :], bk(b)[:, :, 64 * hh:64 * hh + 64], ACT.Copy, after=[m, z2])
                vtiles.append(t)
            free[b] = t
        return m

    drain(gemm([[("wkv", n)] for n in range(4)], XKV, evac_kv))
    vm = kv_post()
    kv_mm = used[-1]
    att = {("L", 1): list(copies.values())}
    qfree = [vm, vm, None]
    ready_q, bfree, ofree = {}, [None, None], {}
    OB = [XF[:, 16 + i, :] for i in range(16)]
    z_done = {}

    def falling(v):
        return bass.AP(v.tensor, v.offset + 127, [list(v.ap[0]), [128, 4], [-1, 128]])

    def gemm_qz(j):
        def ev(n, bank, last):
            if n == 0:
                x = qb[:, j % 3, :]
                e1 = ve.tensor_tensor(falling(x), bank[:].rearrange("p (n c) -> p n c", n=4),
                                      rb[:].rearrange("p (n c) -> p n c", n=4), ALU.mult,
                                      after=[last, qfree[j % 3]])
                ready_q[j] = e1
            else:
                e1 = ve.tensor_tensor(OB[j], bank[:], rb[:], ALU.mult, after=[last, kv_mm])
                z_done[j] = e1
            return e1
        yield from gemm([[("wb", j)], [("wb", 16 + j)]], XB, ev)


    def load_bias(j):
        src = bass.AP(scratch.tensor, 2 * j * 384, [[1, 128], [384, 2], [1, 256]])
        return Q.dma("sync", bsem[j % 2], bias[:, j % 2], src, tab_out, bfree[j % 2])

    bsem = [sem("bias0"), sem("bias1")]
    l_bias = {0: load_bias(0), 1: load_bias(1)}
    qn = {}

    def qnorm(j):
        r = L[:, j % 2].rearrange("p a b c -> p (a b c)")
        qn[j] = head_rms(qb[:, j % 3, :], ready_q[j], C_QB, r[:, 0:512], r[:, 512:1024], "b_q_gain",
                         [att.get(("L", j % 2)), tab_out])

    pend, zs = {}, {}

    def attend(j):
        g, c = j // 4, j % 2
        qn_ = qn[j]
        x = qb[:, j % 3, :]
        Lj = L[:, c]
        mo = []
        for n in range(4):
            b = 4 + n % 2
            lo = 0 if n else 128
            w = 256 - lo
            bb = banks[b][:].rearrange("p (e s) -> p e s", e=2)
            m = pe.matmul(bb[:, :, lo:], x[:, n * 128:(n + 1) * 128],
                          kpad[:, g, :, n * 128 - 128 + lo:n * 128 + 128], start=True, stop=True,
                          after=[qn_, copies[g], free[b]])
            for e in range(2):
                u = 2 * n + e
                o = ve.tensor_tensor_reduce(out=Lj[:, e, n, lo:], in0=bb[:, e, lo:], in1=bias[:, c, e, lo:],
                                            scalar=sinks[:, 2 * j + e:2 * j + e + 1], op0=ALU.add, op1=ALU.max,
                                            accum_out=mx[:, c, u:u + 1],
                                            after=[m, l_bias[j], l_snk, att.get(("L", c)), att.get(("mx", c)), qn_])
            free[b] = o
            mo.append(o)
            yield
        qfree[j % 3] = m
        bfree[c] = o
        if j + 2 < 16:
            l_bias[j + 2] = load_bias(j + 2)
        nm = ve.tensor_scalar(nmx[:, c], mx[:, c], -1.0, None, ALU.mult, after=[mo])
        sk = ve.tensor_tensor(es[:, c].rearrange("p (n e) -> p n e", e=2), nmx[:, c].rearrange("p (n e) -> p n e", e=2),
                              sinks[:, 2 * j:2 * j + 2].unsqueeze(1).to_broadcast([128, 4, 2]), ALU.add,
                              after=[nm, l_snk])
        ps = {}
        pend[j] = ps
        ex = []
        for n in range(4):
            lo = 0 if n else 128
            for e in range(2):
                u = 2 * n + e
                ex.append(ac.activation(Lj[:, e, n, lo:], Lj[:, e, n, lo:], ACT.Exp, bias=nmx[:, c, u:u + 1],
                                        accum_out=den[:, c, u:u + 1], after=[nm, att.get(("mx", c))]))
            yield
        ek = ac.activation(es[:, c], es[:, c], ACT.Exp, after=[sk])
        dn = ve.tensor_tensor(den[:, c], den[:, c], es[:, c], ALU.add, after=[ex, ek])
        rc = ve.reciprocal(den[:, c], den[:, c], after=[dn])
        for n in range(4):
            lo = 0 if n else 128
            for e in range(2):
                u = 2 * n + e
                ps[u] = po.tensor_scalar(Lj[:, e, n, lo:], Lj[:, e, n, lo:], den[:, c, u:u + 1], 1.0,
                                         ALU.mult, ALU.mult, after=[rc, ex])
        att[("mx", c)] = ps[7]
        yield

    def attend2(j):
        g, c = j // 4, j % 2
        Lj, ps = L[:, c], pend[j]
        if j % 2 == 0:
            for jj in (j, j + 1):
                zs[jj] = ac.activation(OB[jj], OB[jj], ACT.Silu, after=[z_done[jj]])
            tables()
        for n in range(4):
            b = xbank()
            first = True
            for kb in ((0, 1) if n else (1,)):
                for e in range(2):
                    m = pe.transpose(bk(b)[:, 2 * kb + e, :], Lj[:, e, n, kb * 128:(kb + 1) * 128], flip[:],
                                     after=[ps[2 * n + e], l_flip, free[b] if first else None])
                    first = False
            k0 = 0 if n else 2
            if n % 2:
                t = ac.activation(pT[:, n, k0:], bk(b)[:, k0:], ACT.Copy, after=[m, att.get(("pT", n))])
            else:
                t = ve.tensor_copy(pT[:, n, k0:], bk(b)[:, k0:], after=[m, att.get(("pT", n))])
            free[b] = t
            ps[("t", n)] = t
            yield
        att[("L", c)] = m
        b = 6 + j % 2
        for n in range(4):
            kbs = (0, 1) if n else (1,)
            for kb in kbs:
                for e in range(2):
                    vb = n - 1 + kb
                    w = vz[:, vb].rearrange("p a d -> p (a d)")
                    s0 = 64 * (2 * g + 1) - 64 * e
                    m = pe.matmul(bk(b)[:, n, :], w[:, s0:s0 + 128], pT[:, n, 2 * kb + e, :],
                                  start=(kb == kbs[0] and e == 0), stop=(kb == 1 and e == 1),
                                  after=[ps[("t", n)], vtiles, free[b]])
            att[("pT", n)] = m
            yield
        o = ve.tensor_tensor(OB[j], banks[b][:], OB[j], ALU.mult, after=[m, zs[j]])
        free[b] = o
        ofree[j] = o
        yield

    def tiles(j):
        yield from gemm_qz(j)
        qnorm(j)

    XOB = [None] * 16

    def split_ob(lo, hi):
        for i in range(lo, hi):
            XOB[i] = (*OH[i], split_tile(OB[i], *OH[i], ofree[i], used[-1]))
            yield

    drain(tiles(0))
    merge(tiles(1), 2, attend(0), None)
    for j in range(16):
        side = tiles(j + 2) if j < 14 else (split_ob(0, 14) if j == 15 else None)
        merge(side, 1, attend2(j), attend(j + 1) if j < 15 else None)
    drain(split_ob(14, 16))
    if stop == "B":
        dumps = [dump(Q, f"OF{i}", OB[i], ofree[i]) for i in range(16)]
        return finish(Q, ctx, loaded[-4:] + dumps)
    hr = list(h_ready)
    norm["acc"] = norm[0] = norm[1] = norm["acc"]
    norm["rb"] = x_last(Q, "vector")
    drain(gemm([[("wbo", 2 * n), ("wbo", 2 * n + 1)] for n in range(8)], XOB, evac_h(hr)))
    if stop == "x2":
        dumps = [dump(Q, f"H{i}", H[:, i, :], h_ready[i]) for i in range(8)]
        return finish(Q, ctx, loaded[-4:] + dumps)
    b_done = [x_last(Q, e) for e in ("vector", "scalar", "tensor", "gpsimd")]

    XC = scaled_split("g_mix_pre", [(slot(k), slot(8 + k)) for k in range(8)], h_ready, used[-1])
    r2 = rstd()
    C = Area(LOC, END)
    qt = C.new([2, 512]); kp = C.new([2, 2, 512]); vst = C.new([512]); vc = C.new([2, 4, 3, 64])
    sp = C.new([2, 3, 512]); am = C.new([2, 2, 512]); spsum = C.new([2, 512])
    yt = C.new([2, 512]); ysq = C.new([512]); yrt = C.new([512])
    up = C.new([528]); ua = C.new([528]); ub = C.new([528]); wpool = C.new([4, 128]); smask = C.new([128])
    l_smask = Q.dma("scalar", "smask", smask[:], d["k_smask"], b_done)
    z3 = po.memset(kp[:], 0.0, after=[b_done])
    z4 = po.memset(vc[:], 0.0, after=[b_done])
    z5 = po.memset(up[:, 0:16], 0.0, after=[b_done])
    z6 = po.memset(ua[:, 0:16], 0.0, after=[b_done])
    z7 = po.memset(ub[:, 0:16], 0.0, after=[b_done])
    l_wp = Q.dma("scalar", "wpool", wpool[:], d["wpool"], b_done)
    Y = [(slot(16 + i), slot(24 + i)) for i in range(8)]
    XY = [None] * 8
    cs = {}

    def gemm_qkv(j):
        p = j % 2

        def ev(n, bank, last):
            if n == 0:
                x = ve.scalar_tensor_tensor(out=qt[:, p], in0=bank[:], scalar=0.125, in1=rb[:], op0=ALU.mult,
                                            op1=ALU.mult, after=[last, r2, b_done, cs.get(("q", p))])
                cs[("lq", j)] = x
            elif n == 1:
                xs = [ve.tensor_tensor(kp[64 * e:64 * e + 64, p, e, :], bank[64 * e:64 * e + 64, :],
                                       rb[64 * e:64 * e + 64, :], ALU.mult,
                                       after=[last, r2, z3, cs.get(("q", p))]) for e in range(2)]
                cs[("lk", j)] = xs
                x = xs[1]
            else:
                x = ve.tensor_tensor(vst[:], bank[:], rb[:], ALU.mult, after=[last, r2, b_done, cs.get("vst")])
                b = 6 + p
                for c in range(4):
                    m = pe.transpose(bk(b)[:, c, :], vst[:, c * 128:(c + 1) * 128], ident[:],
                                     after=[x, l_ident, free[b]])
                cs["vst"] = m
                o = vc[:, p, :, 0:3:2, :]
                t = ac.activation(o, bk(b).rearrange("p c (e d) -> p c e d", e=2), ACT.Copy,
                                  after=[m, z4, cs.get(("q", p))])
                free[b] = t
                cs[("lv", j)] = t
            return x

        yield from gemm([[("wc", j)], [("wc", 4 + j)], [("wc", 8 + j)]], XC, ev)

    def stick(j, e, last_of_pair):
        p = j % 2
        po_b = 6 + p
        pb = banks[po_b]
        zb, ms, xs = {}, {}, {}
        c = e

        def view(i):
            return banks[zb[i]][:, 0:512 - 128 * i]

        def logits(i):
            t0, w = 128 * i, 512 - 128 * i
            b = zb[i] = 2 + 2 * e + i % 2
            z, s_ = view(i), sp[:, c, i % 3, 0:w]
            pe.matmul(z, kp[:, p, e, t0:t0 + 128], qt[:, p, t0:], start=True, stop=False,
                      after=[cs[("lq", j)], cs[("lk", j)], free[b]])
            m = pe.matmul(z[:, 0:128], ident[:], smask[:], start=False, stop=True, after=[l_ident, l_smask])
            a = ac.activation(s_, z, ACT.Abs, after=[m, cs.get(("sp", c, i % 3)), b_done])
            a = ac.activation(s_, s_, ACT.Exp, scale=-1.0, after=[a])
            a = ac.activation(s_, s_, ACT.Ln, bias=const(C_ONE), after=[a])
            ms[i] = ve.scalar_tensor_tensor(out=s_, in0=z, scalar=0.0, in1=s_, op0=ALU.max, op1=ALU.add,
                                            after=[a])

        def weights(i):
            t0, w = 128 * i, 512 - 128 * i
            z, s_, a_ = view(i), sp[:, c, i % 3, 0:w], am[:, c, i % 2, 0:w]
            if i < 3:
                pe.matmul(z[:, 128:], nones[:], spsum[:, c, t0 + 128:], start=False, stop=False,
                          after=[cs[("sum", c)], ms[i], l_nones])
            m = pe.matmul(z, ntri[:], s_, start=False, stop=True, after=[ms[i], l_ntri])
            if i == 3:
                cs[("sum", c)] = ve.tensor_copy(spsum[:, c, t0:], s_, after=[ms[i], cs.get(("sumf", c)), b_done])
            elif i:
                u1 = ve.tensor_tensor(spsum[:, c, t0 + 128:], spsum[:, c, t0 + 128:], s_[:, 128:], ALU.add,
                                      after=[m, cs[("sum", c)]])
                u2 = ve.tensor_copy(spsum[:, c, t0:t0 + 128], s_[:, 0:128], after=[ms[i], cs.get(("sumf", c))])
                cs[("sum", c)] = [u1, u2]
            else:
                cs[("sumf", c)] = m
            cs[("sp", c, i % 3)] = [m, cs[("sum", c)]]
            xs[i] = ac.activation(a_, z, ACT.Exp, after=[m, cs.get(("am", c, i % 2)), b_done])
            free[zb[i]] = xs[i]

        def values(i):
            t0, w = 128 * i, 512 - 128 * i
            wv = vc[:, p, i].rearrange("p a d -> p (a d)")[:, 64 * e:64 * e + 128]
            first = cs.get(("first", j)) is None
            cs[("first", j)] = 1
            m = pe.matmul(pb[:, t0:], wv, am[:, c, i % 2, 0:w], start=first, stop=(last_of_pair and i == 0),
                          after=[xs[i], cs[("lv", j)], free[po_b] if first else None])
            cs[("am", c, i % 2)] = m
            return m

        logits(3)
        yield
        logits(2)
        yield
        weights(3)
        yield
        logits(1)
        yield
        weights(2)
        yield
        values(3)
        yield
        logits(0)
        yield
        weights(1)
        yield
        values(2)
        yield
        weights(0)
        yield
        values(1)
        yield
        m = values(0)
        yield
        if cs.setdefault(("done", j), 0) == 0:
            cs[("done", j)] = 1
            return
        s = ac.activation(ysq[:], pb[:], ACT.Square, after=[m, cs.get("ysq"), b_done])
        b = 2
        mm = pe.matmul(banks[b][:], blk1[:], ysq[:], start=True, stop=True, after=[s, l_blk1, free[b]])
        cs["ysq"] = mm
        a = ac.activation(yrt[:], banks[b][:], ACT.Ln, bias=const(C_EPS), scale=1.0 / 64, after=[mm, cs.get("yrt"), b_done])
        free[b] = a
        a = ac.activation(yrt[:], yrt[:], ACT.Exp, scale=-0.5, after=[a])
        y = ve.scalar_tensor_tensor(out=yt[:, p], in0=pb[:], scalar=gain("g_sb", j), in1=yrt[:], op0=ALU.mult,
                                    op1=ALU.mult, after=[a, s, l_gain["g_sb"], cs.get(("yt", p)), b_done])
        cs["yrt"] = y
        free[po_b] = y
        cs[("q", p)] = [m, y]
        XY[4 + j] = (*Y[4 + j], split_tile(yt[:, p], *Y[4 + j], y, used_bo))
        cs[("yt", p)] = XY[4 + j][2]
        yield

    used_bo = used[-1]

    def two(j):
        a, b = stick(j, 0, False), stick(j, 1, True)
        live = [a, b]
        while live:
            for g in list(live):
                if next(g, g) is g:
                    live.remove(g)
            yield

    def pool(j, bank, last):
        x = ve.tensor_tensor(up[:, 16:], bank[:], rb[:], ALU.mult, after=[last, r2, z5, cs.get("up")])
        src, t = up, x
        for k in range(j + 1):
            dst = ua if k % 2 == 0 else ub
            t = ve.tensor_tensor(dst[:, 16:], src[:, 16:], src[:, 16 - (1 << k):528 - (1 << k)], ALU.add,
                                 after=[t, z6, z7, cs.get("uab")])
            src = dst
        c = ve.tensor_tensor(src[:, 16:32], src[:, 16:32], corr[:, j, :], ALU.mult, after=[t, l_corr])
        dd = ub if src is ua else ua
        t = ve.scalar_tensor_tensor(out=dd[:, 16:], in0=src[:, 16:], scalar=0.5 ** (j + 1), in1=up[:, 16:],
                                    op0=ALU.mult, op1=ALU.subtract, after=[c, t])
        cs["up"] = t
        b = 6
        m = pe.matmul(banks[b][:], wpool[:, j, :], dd[:, 16:], start=True, stop=True, after=[t, l_wp, free[b]])
        cs["uab"] = m
        y = ac.activation(yt[:, j % 2], banks[b][:], ACT.Copy, scale=gain("pool_scale", j),
                          after=[m, l_gain["pool_scale"], cs.get(("yt", j % 2)), b_done])
        free[b] = y
        XY[j] = (*Y[j], split_tile(yt[:, j % 2], *Y[j], y, used_bo))
        cs[("yt", j % 2)] = XY[j][2]
        return x

    def gemm_u():
        yield from gemm([[("wc", 12 + n)] for n in range(4)], XC, pool)

    drain(gemm_qkv(0))
    for j in range(4):
        merge(gemm_qkv(j + 1) if j < 3 else gemm_u(), 2, two(j))
    c_done = [x_last(Q, e) for e in ("vector", "scalar", "tensor", "gpsimd")]

    D = Area(LOC, END)
    xm = D.new([16, 512], R, "xm"); mo = D.new([8, 512])
    XM = [(xm[:, k, :], xm[:, 8 + k, :]) for k in range(8)]

    def evac_mo(n, bank, last):
        t = ac.activation(mo[:, n, :], bank[:], ACT.Copy, after=[last, c_done, cs.get("mo")])
        cs[("mo", n)] = t
        stats(n, mo[:, n, :], t)
        return t

    def post(key):
        r = rstd()
        for n in range(8):
            a = ve.scalar_tensor_tensor(out=mo[:, n, :], in0=mo[:, n, :], scalar=gain(key, n), in1=rb[:],
                                        op0=ALU.mult, op1=ALU.mult, after=[r, cs[("mo", n)], norm["acc"], l_gain[key]])
            h_ready[n] = ve.tensor_tensor(H[:, n, :], H[:, n, :], mo[:, n, :], ALU.add, after=[a, h_ready[n]])
        cs["mo"] = norm["rb"] = h_ready[7]

    norm["rb"] = c_done
    drain(gemm([[("wco", n)] for n in range(8)], XY, evac_mo))
    post("g_mix_post")
    if stop == "h3":
        dumps = [dump(Q, f"H{i}", H[:, i, :], h_ready[i]) for i in range(8)]
        return finish(Q, ctx, loaded[-4:] + dumps)

    for n in range(8):
        stats(n, H[:, n, :], h_ready[n])
    XM_ = scaled_split("g_mlp_pre", XM, h_ready, c_done)
    r3 = rstd()
    hid = [None] * 16
    ft = sqt
    cs["ft0"] = cs["ft1"] = norm["acc"]

    def evac_up(base):
        def f(n, bank, last):
            t = ve.scalar_tensor_tensor(out=ft[:, n % 2, :], in0=bank[:], scalar=0.0, in1=rb[:], op0=ALU.max,
                                        op1=ALU.mult, after=[last, r3, cs[f"ft{n % 2}"], norm[n % 2]])
            a = ac.activation(ft[:, n % 2, :], ft[:, n % 2, :], ACT.Square, after=[t])
            hid[n] = (*OH[n], split_tile(ft[:, n % 2, :], *OH[n], a, base))
            cs[f"ft{n % 2}"] = hid[n][2]
            return t
        return f

    def evac_down0(n, bank, last):
        t = ac.activation(mo[:, n, :], bank[:], ACT.Copy, after=[last, h_ready])
        cs[("mo", n)] = t
        return t

    def evac_down1(n, bank, last):
        t = ve.tensor_tensor(mo[:, n, :], bank[:], mo[:, n, :], ALU.add, after=[last, cs[("mo", n)]])
        cs[("mo", n)] = t
        stats(n, mo[:, n, :], t)
        return t

    for half in range(2):
        drain(gemm([[("wu", 16 * half + n)] for n in range(16)], XM_, evac_up(used[-1])))
        if half:
            norm["acc"] = norm[0] = norm[1] = [norm["acc"], cs["ft0"], cs["ft1"]]
        drain(gemm([[("wd", 16 * half + 2 * n), ("wd", 16 * half + 2 * n + 1)] for n in range(8)], hid,
                   evac_down1 if half else evac_down0))
    norm["rb"] = [norm["acc"], x_last(Q, "vector")]

    post("g_mlp_post")
    if stop == "h4":
        dumps = [dump(Q, f"H{i}", H[:, i, :], h_ready[i]) for i in range(8)]
        return finish(Q, ctx, loaded[-4:] + dumps)
    d_done = [used[-1], h_ready]
    pf = [XF[:, 8 + k, :] for k in range(2)]
    XP = []
    for k in range(2):
        l = Q.dma("scalar", f"p{k}", pf[k], d["p"][k], d_done)
        XP.append((slot(10 + 2 * k), slot(11 + 2 * k), split_tile(pf[k], slot(10 + 2 * k), slot(11 + 2 * k), l)))
    E_ = [XF[:, k, :] for k in range(8)]
    ee = [None] * 8
    for half in range(2):
        i, ah, alo_, ready = block("wp", half)
        ah = wh[:, i % NSPL, :].rearrange("p (n k m) -> p n k m", n=4, k=2)
        alo_ = wl[:, i % NSPL, :].rearrange("p (n k m) -> p n k m", n=4, k=2)
        for n in range(4):
            b = gb_turn[0] % 2
            gb_turn[0] += 1
            for k in range(2):
                last = mm3(banks[b][:], ah[:, n, k, :], alo_[:, n, k, :], XP[k][0], XP[k][1], k == 0, k == 1,
                           ready, XP[k][2], free[b] if k == 0 else None)
            f = 4 * half + n
            ee[f] = ac.activation(E_[f], banks[b][:], ACT.Copy, after=[last, d_done])
            free[b] = ee[f]
            stats(f, E_[f], ee[f])
        used[i] = last
    r4 = rstd()
    for f in range(8):
        ee[f] = ve.scalar_tensor_tensor(out=E_[f], in0=E_[f], scalar=gain("g_ple", f), in1=rb[:],
                                        op0=ALU.mult, op1=ALU.mult, after=[r4, ee[f], norm["acc"], l_gain["g_ple"]])
    XG = []
    for k in range(8):
        XG.append((*XM[k], split_tile(H[:, k, :], *XM[k], h_ready[k], d_done)))
    stores = []

    def evac_gate(n, bank, last):
        s = ac.activation(mo[:, n, :], bank[:], ACT.Sigmoid, after=[last, d_done])
        t = ve.tensor_tensor(mo[:, n, :], mo[:, n, :], E_[n], ALU.mult, after=[s, ee[n]])
        t = ve.tensor_tensor(mo[:, n, :], mo[:, n, :], H[:, n, :], ALU.add, after=[t, h_ready[n]])
        stores.append(Q.dma("scalar", f"out{n}", out[n], mo[:, n, :], t))
        return s

    drain(gemm([[("wg", n)] for n in range(8)], XG, evac_gate))
    return finish(Q, ctx, stores)

    return finish(Q, ctx, loaded[-4:])


def x_last(q, eng):
    return q.q[eng][-1]


def chain(*gens):
    for g in gens:
        yield from g


def spread(g, every):
    for _ in g:
        for _ in range(every - 1):
            yield "pass"
        yield


def drain(gen):
    for _ in gen:
        pass


def merge(g, n, *others, later=None):
    live = [x for x in others if x is not None]
    credit = 0
    while g is not None or live:
        for x in list(live) or [None]:
            if x is not None:
                r = next(x, x)
                if r is x:
                    live.remove(x)
                elif r == "pass":
                    continue
            credit += n
            if later:
                later.pop(0)()
            while credit >= 1:
                credit -= 1
                if g is not None and next(g, g) is g:
                    g = None
    while later:
        later.pop(0)()


def finish(Q, ctx, stores=()):
    Q.op("sync", lambda e: e.nop(), *stores)
    Q.count()
    block = ctx.enter_context(Q.nc.Block())
    block.sync(lambda e: Q.emit("sync", e))
    block.gpsimd(lambda e: Q.emit("gpsimd", e))
    block.scalar(lambda e: Q.emit("scalar", e))
    block.vector(lambda e: Q.emit("vector", e))
    block.tensor(lambda e: Q.emit("tensor", e))


_N_BUCKETS, _MAX_DIST = 32, 128


def _bucket(dist):
    import numpy as np

    n = np.maximum(dist, 0)
    exact = _N_BUCKETS // 2
    large = exact + (np.log(np.maximum(n, 1) / exact) / np.log(_MAX_DIST / exact)
                     * (_N_BUCKETS - exact)).astype(np.int64)
    return np.where(n < exact, n, np.minimum(large, _N_BUCKETS - 1)).astype(np.int32)


def constants():
    import numpy as np

    f = np.float32
    i = np.arange(128)
    c = {}
    c["k_ident"] = np.eye(128, dtype=f)
    c["k_triu"] = (i[:, None] <= i[None, :]).astype(f)
    c["k_ones"] = np.ones((128, 128), f)
    c["k_blk1"] = (i[:, None] // 64 == i[None, :] // 64).astype(f)
    c["k_ntri"] = -(i[:, None] >= i[None, :]).astype(f)
    c["k_nones"] = -np.ones((128, 128), f)
    c["k_flip"] = np.ascontiguousarray(np.eye(128, dtype=f)[::-1])
    c["k_smask"] = np.where(i[:, None] >= i[None, :], -1.0e30, 0.0).astype(f)
    m = np.zeros((128, 7, 128), f)
    for n in range(7):
        b = 1 << n
        m[:, n, :] = ((i[:, None] // (2 * b) == i[None, :] // (2 * b)) & (i[:, None] // b < i[None, :] // b))
    c["k_masks"] = m
    cc = np.zeros((128, 8), f)
    cc[:, 0] = 1e-6
    cc[:, 1] = -0.5 * np.log(128.0)
    cc[:, 2] = -0.5 * np.log(64.0)
    cc[:, 3] = 1.0
    c["k_cc"] = cc
    corr = np.ones((128, 4, 16), f)
    for n, w in enumerate((2, 4, 8, 16)):
        corr[:, n, :] = w / np.minimum(np.arange(16) + 1, w)
    c["k_corr"] = corr
    j = np.arange(384)
    dist = 255 - j
    ok = (dist >= 0) & (dist < 128)
    hot = np.zeros((32, 384), f)
    hot[_bucket(dist), j] = ok
    c["k_hot"] = hot
    c["k_neg"] = np.where(ok, 0.0, -1.0e30).astype(f)[None].repeat(32, 0)
    return c


def layout(i):
    import numpy as np

    a = {k: np.asarray(v) for k, v in i.items()}

    def blocks(w):
        k, n = w.shape
        return np.ascontiguousarray(w.reshape(k // 1024, 8, 128, n // 128, 128).transpose(3, 0, 2, 1, 4)
                                    .reshape(-1, 128, 1024))

    def col(v):
        return np.ascontiguousarray(v.reshape(-1, 128).T)

    w = a["a_w_in"][0]
    tiles = []
    for h in range(8):
        tiles += [w[:, h * 128:h * 128 + 128], w[:, 1024 + h * 128:1152 + h * 128],
                  w[:, 2048 + h * 256:2304 + h * 256], w[:, 4096 + h * 256:4352 + h * 256]]
    d = {}
    d["wa"] = blocks(np.concatenate(tiles, axis=1))
    d["wab"] = np.ascontiguousarray(w[:, 6144:6160].reshape(8, 128, 16).transpose(1, 0, 2))
    d["x"] = np.ascontiguousarray(a["x"][0].T.reshape(8, 128, 512))
    d["a_conv"] = np.ascontiguousarray(a["a_conv"][0].reshape(4, 32, 128).transpose(2, 0, 1))
    al = np.stack([a["a_A_log"][0], a["a_dt_bias"][0]])
    d["alog"] = np.ascontiguousarray(np.broadcast_to(al[None], (128, 2, 8)))
    d["wao"] = blocks(a["a_w_out"][0])
    d["wkv"] = blocks(a["w_kv"])
    d["wb"] = blocks(a["b_w_in"][0])
    d["wbo"] = blocks(a["b_w_out"][0])
    wc = a["w_in_2"][0]
    d["wc"] = blocks(np.concatenate([wc[:, 512:], wc[:, :512]], axis=1))
    wp = a["w_ple_proj_2"][0]
    d["wp"] = np.ascontiguousarray(wp.reshape(2, 128, 2, 4, 128).transpose(2, 1, 3, 0, 4).reshape(2, 128, 1024))
    d["wco"] = blocks(a["w_out_2"][0])
    d["wu"] = blocks(a["w_up_2"][0])
    wd = a["w_down_2"][0]
    d["wd"] = np.concatenate([blocks(wd[:2048]), blocks(wd[2048:])])
    d["wg"] = blocks(a["w_ple_gate_2"][0])
    d["wpool"] = np.ascontiguousarray(a["w_pool_2"][0].transpose(1, 0, 2))
    d["p"] = np.ascontiguousarray(a["p_2"][0, 0].T.reshape(2, 128, 512))
    d["rel"] = a["rel_bias"]
    d["sinks"] = np.ascontiguousarray(np.broadcast_to(a["b_sinks"].reshape(1, 32), (128, 32)))
    for key, src in (("a_norm", "a_norm"), ("kv_norm", "kv_norm"), ("b_norm", "b_norm"),
                     ("g_mix_pre", "g_mix_pre_2"), ("g_mix_post", "g_mix_post_2"), ("g_mlp_pre", "g_mlp_pre_2"),
                     ("g_mlp_post", "g_mlp_post_2"), ("g_ple", "g_ple_2"), ("g_sb", "g_sb_2"),
                     ("pool_scale", "pool_scale_2"), ("a_o_gain", "a_o_gain")):
        d[key] = col(a[src])
    for key, src in (("k_gain", "k_gain"), ("b_q_gain", "b_q_gain")):
        v = a[src].reshape(1, 64)
        d[key] = np.ascontiguousarray(np.concatenate([v, v], axis=1).reshape(128, 1))
    return d


def kernel(**inputs):
    import numpy as _np
    import concourse.bacc as _bacc
    from concourse import mybir as _mybir
    from concourse.bass_utils import run_bass_kernel_spmd as _run

    nc = _bacc.Bacc("TRN2", target_bir_lowering=False, num_devices=1)
    given = {**layout(inputs), **constants()}
    arrays, args = {}, {}
    for name, a in given.items():
        a = _np.ascontiguousarray(a)
        arrays["in_" + name] = a
        args[name] = nc.dram_tensor("in_" + name, a.shape, _mybir.dt.from_np(a.dtype), kind="ExternalInput").ap()
    out = nc.dram_tensor("out_0_dram", (8, 128, 512), _mybir.dt.float32, kind="ExternalOutput").ap()
    program(nc, args, out)
    r = _run(nc, [arrays], core_ids=[0])
    got = r.results[0]["out_0_dram"]
    return _np.ascontiguousarray(got.reshape(1024, 512).T).reshape(1, 512, 1024)
```

```python
from contextlib import ExitStack
from functools import partial

import numpy as np

import concourse.bass as bass
from concourse import mybir

F = mybir.dt.float32
R = mybir.dt.float32r
ACT = mybir.ActivationFunctionType
ALU = mybir.AluOpType
AX = mybir.AxisListType

T = 512
EPS = 1e-6
KB = 1024
SB0 = 16512

C_EPS, C_QA, C_QB, C_ONE, C_ZERO = range(5)
N_CC = 8

HEADS = 8

GAINS = (("a_norm", 8), ("kv_norm", 8), ("b_norm", 8), ("g_mix_pre", 8), ("g_mix_post", 8), ("g_mlp_pre", 8),
         ("g_mlp_post", 8), ("g_ple", 8), ("g_sb", 4), ("pool_scale", 4), ("a_o_gain", 2), ("k_gain", 1),
         ("b_q_gain", 1))
N_GAIN = 76


def block_order():
    out = []
    for i in range(HEADS + 2):
        if i >= 2:
            out += [("wa", (i - 2) * 6 + j) for j in (4, 5)]
        if i < HEADS:
            out += [("wa", i * 6 + j) for j in range(4)]
    out += [("wao", b) for b in range(16)]
    out += [("wkv", b) for b in range(4)]
    for j in range(16):
        out += [("wb", j), ("wb", 16 + j)]
    out += [("wbo", b) for b in range(16)]
    for j in range(4):
        out += [("wc", 15 - j)] if j else []
        out += [("wc", j), ("wc", 4 + j), ("wc", 8 + j)]
        out += [("wc", 15)] if j == 0 else []
    out += [("wco", b) for b in range(8)]
    for half in range(2):
        out += [("wu", 16 * half + b) for b in range(16)]
        out += [("wd", 16 * half + b) for b in range(16)]
    out += [("wp", b) for b in range(2)]
    out += [("wg", b) for b in range(8)]
    return out


class Op:

    __slots__ = ("eng", "fn", "deps", "used", "sem", "val")

    def __init__(self, eng, fn, deps, sem=None, val=0):
        self.eng, self.fn, self.deps, self.sem, self.val = eng, fn, deps, sem, val
        self.used = False


class Queues:

    ENGINES = ("sync", "gpsimd", "scalar", "vector", "tensor")

    def __init__(self, nc, sem):
        self.nc, self.newsem = nc, sem
        self.q = {e: [] for e in self.ENGINES}
        self.sems = {e: sem("s_" + e) for e in self.ENGINES}
        self.counts = {}

    def op(self, eng, fn, *deps):
        flat, todo = [], list(deps)
        while todo:
            x = todo.pop()
            if type(x) in (list, tuple):
                todo += x
            elif x is not None:
                flat.append(x)
        for d in flat:
            d.used = True
        o = Op(eng, fn, flat)
        self.q[eng].append(o)
        return o

    def dma(self, eng, sem, out, in_, *deps):
        if isinstance(sem, str):
            sem = self.newsem(sem)
        o = self.op(eng, lambda e: e.dma_start(out, in_), *deps)
        n = self.counts.get(sem.name, 0) + 16
        self.counts[sem.name] = n
        o.sem, o.val = sem, n
        return o

    def count(self):
        for e in self.ENGINES:
            n = 0
            for o in self.q[e]:
                if o.sem is None and o.used:
                    n += 1
                    o.val = n

    def emit(self, eng, e):
        seen = {}
        for o in self.q[eng]:
            need = {}
            for d in o.deps:
                s = d.sem if d.sem is not None else self.sems[d.eng]
                if d.val > seen.get(s.name, 0):
                    if s.name not in need or need[s.name][1] < d.val:
                        need[s.name] = (s, d.val)
            for name, (s, v) in need.items():
                e.wait_ge(s, v)
                seen[name] = v
            ins = o.fn(e)
            if o.sem is not None:
                ins.then_inc(o.sem, 16)
            elif o.used:
                ins.then_inc(self.sems[eng], 1)


class Tensor:

    def __init__(self, q):
        self.q = q

    def matmul(self, out, w, x, start, stop, after=()):
        return self.q.op("tensor", lambda e: e.matmul(out, w, x, start=start, stop=stop, skip_group_check=True),
                         *after)

    def transpose(self, out, x, ident, after=()):
        return self.q.op("tensor", lambda e: e.transpose(out, x, ident), *after)


class Vector:

    def __init__(self, q, eng="vector"):
        self.q, self.eng = q, eng

    def tensor_tensor(self, out, a, b, op, after=()):
        return self.q.op(self.eng, lambda e: e.tensor_tensor(out, a, b, op), *after)

    def tensor_scalar(self, out, a, s1, s2, op0, op1=None, after=()):
        if op1 is None:
            return self.q.op(self.eng, lambda e: e.tensor_scalar(out, a, s1, s2, op0), *after)
        return self.q.op(self.eng, lambda e: e.tensor_scalar(out, a, s1, s2, op0, op1), *after)

    def scalar_tensor_tensor(self, out, in0, scalar, in1, op0, op1, after=()):
        return self.q.op(self.eng, lambda e: e.scalar_tensor_tensor(out=out, in0=in0, scalar=scalar, in1=in1,
                                                                    op0=op0, op1=op1), *after)

    def tensor_tensor_reduce(self, out, in0, in1, scalar, op0, op1, accum_out, after=()):
        return self.q.op(self.eng, lambda e: e.tensor_tensor_reduce(out=out, in0=in0, in1=in1, scale=1.0, scalar=scalar,
                                                                    op0=op0, op1=op1, accum_out=accum_out), *after)

    def tensor_copy(self, out, a, after=()):
        return self.q.op(self.eng, lambda e: e.tensor_copy(out, a), *after)

    def reciprocal(self, out, a, after=()):
        return self.q.op(self.eng, lambda e: e.reciprocal(out, a), *after)

    def memset(self, out, v, after=()):
        return self.q.op(self.eng, lambda e: e.memset(out, v), *after)

    def affine_select(self, out, in_, compare_op, fill, base, pattern, channel_multiplier, after=()):
        return self.q.op(self.eng, lambda e: e.affine_select(out=out, in_=in_, compare_op=compare_op, fill=fill,
                                                             base=base, pattern=pattern,
                                                             channel_multiplier=channel_multiplier), *after)


class Scalar:

    def __init__(self, q):
        self.q = q

    def activation(self, out, x, func, bias=0.0, scale=1.0, accum_out=None, after=()):
        if accum_out is not None:
            return self.q.op("scalar", lambda e: e.activation(out, x, func, bias=bias, scale=scale,
                                                              accum_out=accum_out), *after)
        return self.q.op("scalar", lambda e: e.activation(out, x, func, bias=bias, scale=scale), *after)

    def preload_act_table_set(self, name):
        return self.q.op("scalar", lambda e: e.preload_act_table_set(name))


def program(nc, d, out, dump=None, stop=None):
    ctx = ExitStack()
    with ctx:
        build(nc, d, out, ctx, dump, stop)


def build(nc, d, out, ctx, dump, stop):
    def sem(n):
        return ctx.enter_context(nc.semaphore(n))

    Q = Queues(nc, sem)
    pe, ve, ac, po = Tensor(Q), Vector(Q), Scalar(Q), Vector(Q, "gpsimd")

    top = [SB0]
    names = [0]

    def at(off, shape, dt=F, name="t"):
        names[0] += 1
        return nc.alloc_sbuf_tensor_at(f"{name}{names[0]}", [128] + list(shape), dt, offset=off)

    def size(shape):
        return (int(np.prod(shape)) * 4 + 31) // 32 * 32

    def new(shape, dt=F, name="t"):
        off = top[0]
        top[0] += size(shape)
        assert top[0] <= 229344, top[0]
        return at(off, shape, dt, name)

    class Area:

        def __init__(self, lo, hi):
            self.lo, self.p, self.hi = lo, lo, hi

        def new(self, shape, dt=F, name="a"):
            off = self.p
            self.p += size(shape)
            assert self.p <= self.hi, (self.p, self.hi)
            return at(off, shape, dt, name)

    banks = [ctx.enter_context(nc.psum_tensor(f"ps{i}", [128, 512], F)) for i in range(8)]
    free = [None] * 8

    k1 = new([6 * 128 + N_CC + 64]); masks = new([7, 128]); gains = new([N_GAIN + 128])
    ident, triu, ones, blk1, ntri, nones = (k1[:, 128 * n:128 * n + 128] for n in range(6))
    cc = k1[:, 768:768 + N_CC]
    corr = k1[:, 768 + N_CC:].rearrange("p (a b) -> p a b", a=4)
    convw = gains[:, N_GAIN:].rearrange("p (a b) -> p a b", a=4)
    l_g = Q.dma("scalar", "c_gains", gains[:], d["gains"])
    l_k1 = Q.dma("scalar", "c_k1", k1[:], d["k_k1"])
    l_masks = Q.dma("gpsimd", "c_masks", masks[:], d["k_masks"])
    l_ident = l_triu = l_ones = l_blk1 = l_ntri = l_nones = l_cc = l_corr = l_k1
    l_conv = l_g
    gcol, l_gain = {}, {}
    o = 0
    for key, n in GAINS:
        gcol[key] = gains[:, o:o + n]
        l_gain[key] = l_g
        o += n

    def gain(key, i):
        return gcol[key][:, i:i + 1]

    def const(i):
        return cc[:, i:i + 1]

    NRAW, NSPL = 4, 4
    raw = new([NRAW, 1024], F, "wraw")
    wh = new([NSPL, 1024], R, "wh")
    wl = new([NSPL, 1024], R, "wl")
    order = block_order()
    rawsem = [sem(f"wr{i}") for i in range(NRAW)]
    loaded, split_lo, used = [], [], []
    AHEAD = 2

    def load(j):
        key, b = order[j]
        loaded.append(Q.dma("sync", rawsem[j % NRAW], raw[:, j % NRAW, :], d[key][b],
                            split_lo[j - NRAW] if j >= NRAW else None))

    def split(i):
        while len(loaded) < min(len(order), i + 1):
            load(len(loaded))
        r, h, lo = raw[:, i % NRAW, :], wh[:, i % NSPL, :], wl[:, i % NSPL, :]
        gone = used[i - NSPL] if i >= NSPL else None
        hi = ac.activation(h, r, ACT.Copy, after=[loaded[i], gone])
        split_lo.append(ve.tensor_tensor(lo, r, h.bitcast(F), ALU.subtract, after=[hi, gone, loaded[i]]))
        while len(loaded) < min(len(order), i + NRAW + 1):
            load(len(loaded))

    def block(key, b):
        i = len(used)
        assert order[i] == (key, b), (i, order[i], key, b)
        oldest = next((n for n in range(max(0, i - NSPL), i) if used[n] is None), i)
        while len(split_lo) < min(len(order), i + 1 + AHEAD, oldest + NSPL):
            split(len(split_lo))
        used.append(None)
        v = lambda w: w[:, i % NSPL, :].rearrange("p (k n) -> p k n", n=128)
        return i, v(wh), v(wl), split_lo[i]

    def ahead(n):
        while len(split_lo) < min(len(order), len(used) + n):
            split(len(split_lo))

    def mm3(bank, wa, wb, xa, xb, first, last, *deps):
        pe.matmul(bank, wa, xa, start=first, stop=False, after=[*deps])
        pe.matmul(bank, wa, xb, start=False, stop=False)
        return pe.matmul(bank, wb, xa, start=False, stop=last)

    WIDE, NARROW = [0, 1, 4, 5, 6, 7], [0, 1]
    ring = {"banks": WIDE, "turn": 0}

    def use_banks(v):
        ring["banks"], ring["turn"] = v, 0

    def next_bank():
        ring["turn"] += 1
        return ring["banks"][(ring["turn"] - 1) % len(ring["banks"])]

    def gemm(keys, X, evac, wide=0):
        if wide:
            got = [(block(*keys[n][0]), next_bank()) for n in range(wide)]
            lasts = []
            for k in range(8):
                xh, xl, xr = X[k]
                for (i, ah, al, ready), b in got:
                    last = mm3(banks[b][:], ah[:, k, :], al[:, k, :], xh, xl, k == 0, k == 7,
                               ready if k == 0 else None, xr, free[b] if k == 0 else None)
                    if k == 7:
                        used[i] = last
                        lasts.append(last)
                    yield
            ahead(2)
            for n, (_, b) in enumerate(got):
                free[b] = evac(n, banks[b], lasts[n])
                yield
        for n, blocks in enumerate(keys[wide:], wide):
            b = next_bank()
            k, total = 0, 8 * len(blocks)
            for key, j in blocks:
                i, ah, al, ready = block(key, j)
                for kk in range(8):
                    xh, xl, xr = X[k]
                    last = mm3(banks[b][:], ah[:, kk, :], al[:, kk, :], xh, xl, k == 0, k == total - 1,
                               ready if kk == 0 else None, xr, free[b] if k == 0 else None)
                    k += 1
                    if kk == 7:
                        used[i] = last
                    yield
            free[b] = evac(n, banks[b], last)
            yield

    def split_tile(src, hi, lo, *deps, scale=None):
        a = ac.activation(hi, src, ACT.Copy, after=[*deps])
        return [a, ve.tensor_tensor(lo, src, hi.bitcast(F), ALU.subtract, after=[a, *deps])]

    xreg = new([32, 512], F, "xreg")
    xoff = top[0] - 64 * KB
    XR = at(xoff, [32, 512], R, "xr")
    XF = xreg
    HOFF = top[0]
    H = new([8, 512], F, "h")
    LOC = top[0]
    END = 229344

    def rms(sq_acc, n, bank_i, tmp, rb, dep, eps_scale):
        m = pe.matmul(banks[bank_i][:], ones, sq_acc, start=True, stop=True, after=[dep, l_ones, free[bank_i]])
        a = ac.activation(tmp, banks[bank_i][:], ACT.Ln, bias=const(C_EPS), scale=eps_scale, after=[m, l_cc, n])
        free[bank_i] = a
        return ac.activation(rb, tmp, ACT.Exp, scale=-0.5, after=[a, n])

    tables = lambda: ac.preload_act_table_set("natural_log_exp_and_others")
    tables()

    A = Area(HOFF, END)
    x_in = [XF[:, 16 + k, :] for k in range(8)]
    ldx = []
    for k in range(8):
        ldx.append(Q.dma("sync", f"x{k}", x_in[k], d["x"][k]))
        if k in (0, 2, 4):
            load(k // 2)
    rb = A.new([512]); rtmp = A.new([512]); sqa = A.new([512]); sqt = A.new([2, 512])
    XA = []
    acc = ve.memset(sqa[:], 0.0)
    sqfree = [None, None]
    for k in range(8):
        if k in (1, 2, 4):
            split(k // 2)
        xh, xl = XR[:, k, :], XR[:, 8 + k, :]
        s = ac.activation(sqt[:, k % 2, :], x_in[k], ACT.Square, after=[ldx[k], sqfree[k % 2]])
        acc = ve.tensor_tensor(sqa[:], sqa[:], sqt[:, k % 2, :], ALU.add, after=[s, acc])
        sqfree[k % 2] = acc
        g = gain("a_norm", k)
        hi = ac.activation(xh, x_in[k], ACT.Copy, scale=g, after=[ldx[k], l_gain["a_norm"]])
        lo = ve.scalar_tensor_tensor(
            out=xl, in0=x_in[k], scalar=g, in1=xh.bitcast(F), op0=ALU.mult, op1=ALU.subtract, after=[hi, ldx[k]])
        XA.append((xh, xl, [hi, lo]))
    cin = A.new([2, 516])
    cz = ve.memset(cin[:], 0.0)
    cfree = [cz, cz]
    qkv = A.new([2, 4, 512]); zb = A.new([2, 512])
    qkv_free = [None, None]
    z_free = [None, None]
    sqh = A.new([2, 512]); rq = A.new([2, 512])
    qd = A.new([2, 512]); qf = [None, None]
    kg = A.new([4, 128])
    kd = A.new([2, 4, 128]); vt = A.new([2, 4, 256]); wT = A.new([2, 4, 128])
    U = A.new([2, 4, 128]); qkT = A.new([2, 4, 128])
    Dm = A.new([4, 128]); AT = A.new([4, 128]); Tm = A.new([4, 128]); Pm = A.new([4, 128]); Mm = A.new([2, 4, 128])
    S = A.new([2, 256]); rr = rtmp[:].rearrange("p (a b) -> p a b", a=2); ot = sqt; osq = sqh
    state = {}
    OF = [XF[:, 16 + i, :] for i in range(16)]
    of_done = [None] * 16
    pre = {}

    later, taps = [], [0, 0]

    def conv(h, ch, j, bank, last):
        b = state.setdefault("cin", 0) % 2
        while taps[b]:
            later.pop(0)()
        state["cin"] += 1
        src, dst = cin[:, b, :], qkv[:, h % 2, j, :]
        ev = ve.tensor_tensor(src[:, 3:515], bank[:], rb[:], ALU.mult, after=[last, rdone, cfree[b]])
        t = ac.activation(dst, src[:, 3:515], ACT.Copy, scale=convw[:, 3, ch:ch + 1], after=[ev, l_conv, qkv_free[h % 2]])
        cfree[b] = t
        mine = pre.setdefault(h, [None] * 4)
        mine[j] = t

        def tap(w):
            cfree[b] = mine[j] = ve.scalar_tensor_tensor(out=dst, in0=src[:, w:w + 512], scalar=convw[:, w, ch:ch + 1],
                                                         in1=dst, op0=ALU.mult, op1=ALU.add,
                                                         after=[mine[j], ev, l_conv])
            taps[b] -= 1

        taps[b] = 3
        for w in range(3):
            later.append(partial(tap, w))
        return ev

    def gemm_head(h):
        yield from gemm([[("wa", 6 * h + j)] for j in range(4)], XA,
                        lambda n, bank, last: conv(h, [h, 8 + h, 16 + 2 * h, 17 + 2 * h][n], n, bank, last),
                        wide=0 if h else 3)

    def gemm_z(h):
        zs = []

        def ev(n, bank, last):
            e1 = ve.tensor_tensor(zb[:, n, :], bank[:], rb[:], ALU.mult, after=[last, rdone, z_free[n]])
            zs.append(e1)
            return e1

        yield from gemm([[("wa", 6 * h + 4 + j)] for j in range(2)], XA, ev)
        state[("z", h)] = zs

    woff = xoff + 31 * 2 * KB
    wab, wabh, wabl = (at(woff + 512 * n, [8, 16], t, "wab") for n, t in enumerate((F, R, R)))
    lw = Q.dma("scalar", "wab", wab[:], d["wab"])
    al = A.new([2, 8])
    lal = Q.dma("scalar", "alog", al[:], d["alog"])
    ab = A.new([4, 16])
    s1 = A.new([4, 8]); s2 = A.new([4, 8]); s3 = A.new([4, 8]); lnb = A.new([8, 4])
    gg = A.new([8, 4])
    gcum = A.new([32]); glast = A.new([32]); gsub = A.new([32]); egn = A.new([32]); ekd = A.new([32]); egl = A.new([32])
    gt = {}

    def gates():
        h1 = ac.activation(wabh[:], wab[:], ACT.Copy, after=[lw])
        h2 = ve.tensor_tensor(wabl[:], wab[:], wabh[:].bitcast(F), ALU.subtract, after=[h1, lw])
        for k in range(8):
            xh, xl, xr = XA[k]
            m = mm3(banks[7][0:16, :], wabh[:, k, :], wabl[:, k, :], xh, xl, k == 0, k == 7, xr, h1, h2)
        abT = rtmp[0:16, :]
        e0 = ve.tensor_tensor(abT, banks[7][0:16, :], rb[0:16, :], ALU.mult, after=[m, rdone])
        free[7] = e0
        yield
        for n in range(4):
            m = pe.transpose(banks[3][:, n * 16:n * 16 + 16], rtmp[0:16, n * 128:(n + 1) * 128], ident[0:16, 0:16],
                             after=[e0, l_ident])
        e0 = ve.tensor_copy(ab[:], banks[3][:, 0:64].rearrange("p (n c) -> p n c", n=4), after=[m])
        free[3] = e0
        bl, alo = ab[:, :, 0:8], ab[:, :, 8:16]
        t = ac.activation(s1[:], bl, ACT.Abs, after=[e0])
        t = ac.activation(s1[:], s1[:], ACT.Exp, scale=-1.0, after=[t])
        t = ac.activation(s1[:], s1[:], ACT.Ln, bias=const(C_ONE), after=[t])
        t_lnb = ve.scalar_tensor_tensor(out=lnb[:].rearrange("p h n -> p n h"), in0=bl, scalar=0.0, in1=s1[:],
                                        op0=ALU.min, op1=ALU.subtract, after=[t])
        yield
        t = ve.tensor_tensor(s2[:], alo, al[:, 1, :].unsqueeze(1).to_broadcast([128, 4, 8]), ALU.add, after=[lal, e0])
        t1 = ac.activation(s3[:], s2[:], ACT.Abs, after=[t])
        t1 = ac.activation(s3[:], s3[:], ACT.Exp, scale=-1.0, after=[t1])
        t1 = ac.activation(s3[:], s3[:], ACT.Ln, bias=const(C_ONE), after=[t1])
        t2 = ac.activation(al[:, 0, :], al[:, 0, :], ACT.Exp, after=[lal])
        t = ve.scalar_tensor_tensor(out=s2[:], in0=s2[:], scalar=0.0, in1=s3[:], op0=ALU.max, op1=ALU.add, after=[t1])
        t_g = ve.scalar_tensor_tensor(out=gg[:].rearrange("p h n -> p n h"), in0=s2[:], scalar=-1.0,
                                      in1=al[:, 0, :].unsqueeze(1).to_broadcast([128, 4, 8]),
                                      op0=ALU.mult, op1=ALU.mult, after=[t, t2])
        yield
        yield
        g32 = gg[:].rearrange("p h n -> p (h n)")
        m1 = pe.matmul(banks[2][:, 0:32], triu, g32, start=True, stop=True, after=[t_g, l_triu, free[2]])
        m2 = pe.matmul(banks[3][:, 0:32], ones, g32, start=True, stop=True, after=[t_g, free[3]])
        v1 = ve.tensor_copy(gcum[:], banks[2][:, 0:32], after=[m1])
        v2 = ve.tensor_copy(glast[:], banks[3][:, 0:32], after=[m2])
        free[2], free[3] = v1, v2
        l32 = lnb[:].rearrange("p h n -> p (h n)")
        t_gs = ve.tensor_tensor(gsub[:], gcum[:], l32, ALU.subtract, after=[v1, t_lnb])
        t = ac.activation(egn[:], gcum[:], ACT.Exp, after=[v1])
        t_egn = ve.tensor_scalar(egn[:], egn[:], -1.0, None, ALU.mult, after=[t])
        t = ve.tensor_tensor(ekd[:], glast[:], gsub[:], ALU.subtract, after=[v2, t_gs])
        t_ekd = ac.activation(ekd[:], ekd[:], ACT.Exp, after=[t])
        t_egl = ac.activation(egl[:], glast[:], ACT.Exp, after=[v2])
        gt.update(g=t_g, gs=t_gs, egn=t_egn, ekd=t_ekd, egl=t_egl)
        yield

    first = gemm_head(0)
    for _ in range(24):
        next(first)
    rdone = rms(sqa[:], None, 2, rtmp[:], rb[:], acc, 1.0 / 1024)

    def bk(i):
        return banks[i][:].rearrange("p (n c) -> p n c", n=4)

    turn = [0]

    def xbank():
        turn[0] += 1
        return 2 + turn[0] % 2

    def bc(v, w=128):
        return v.unsqueeze(2).to_broadcast([128, 4, w])

    def prep(h):
        p = h % 2
        col = slice(4 * h, 4 * h + 4)
        b = xbank()
        for n in range(4):
            m = pe.matmul(bk(b)[:, n, :], gg[:, h, n:n + 1].to_broadcast([128, 128]), triu,
                                                start=True, stop=True, after=[free[b] if n == 0 else None, gt["g"], l_triu])
        yield
        dv = ve.tensor_tensor(Dm[:], bk(b), bc(gsub[:, col]), ALU.subtract, after=[m, gt["gs"], state.get("Dfree")])
        egb = rq[:, 1, :]
        sel = po.affine_select(out=Dm[:], in_=Dm[:], compare_op=ALU.is_ge, fill=-1.0e4, base=0,
                               pattern=[[0, 4], [1, 128]], channel_multiplier=-1, after=[dv])
        silus, sqs = [], []
        for j in range(2):
            v = qkv[:, p, j, :]
            silus.append(ac.activation(v, v, ACT.Silu, after=[pre[h][j]]))
        for j in range(2):
            sqs.append(ac.activation(sqh[:, j, :], qkv[:, p, j, :], ACT.Square,
                                     after=[silus[j], state.get(("sqh", j))]))
        for j in range(2, 4):
            v = qkv[:, p, j, :]
            silus.append(ac.activation(v, v, ACT.Silu, after=[pre[h][j]]))
        tables()
        yield
        yield
        yield
        q, k = qkv[:, p, 0, :], qkv[:, p, 1, :]
        norm, sums = [], []
        for j in range(2):
            c = xbank()
            m = pe.matmul(banks[c][:], ones, sqh[:, j, :], start=True, stop=True, after=[sqs[j], free[c]])
            state[("sqh", j)] = m
            sums.append((c, m))
            if j == 0:
                eb = ac.activation(egb, banks[b][:], ACT.Exp, after=[dv, state.get("rqfree")])
                free[b] = [dv, eb]
                yield
        for j, v in enumerate((q, k)):
            c, m = sums[j]
            l = ac.activation(rq[:, 0, :], banks[c][:], ACT.Ln, bias=const(C_EPS), after=[m, state.get("rq0"), l_cc])
            free[c] = l
            x = ac.activation(rq[:, 0, :], rq[:, 0, :], ACT.Exp, scale=-0.5,
                              bias=const(C_QA) if j == 0 else const(C_ZERO), after=[l])
            y = ve.tensor_tensor(v, v, rq[:, 0, :], ALU.mult, after=[x, silus[j]])
            state["rq0"] = y
            norm.append(y)
            yield
            yield
        E = ac.activation(Dm[:], Dm[:], ACT.Exp, after=[sel])
        qdn = ve.tensor_tensor(qd[:, p, :], q, egb, ALU.mult, after=[norm[0], eb, qf[p]])
        state["rqfree"] = qdn
        b = xbank()
        ch = [slice(n * 128, (n + 1) * 128) for n in range(4)]
        for n in range(4):
            m = pe.matmul(bk(b)[:, n, :], k[:, ch[n]], k[:, ch[n]], start=True, stop=True, after=[norm[1], free[b] if n == 0 else None])
        at_ = ve.tensor_tensor(AT[:], bk(b), Dm[:], ALU.mult, after=[m, E, state.get("ATfree")])
        free[b] = at_
        def level(i, dep):
            s = Mm[:, i % 2]
            return po.tensor_tensor(s, AT[:], masks[:, i, :].unsqueeze(1).to_broadcast([128, 4, 128]),
                                                ALU.mult, after=[dep, l_masks])
        mk = level(0, [at_, state.get("Mfree1")])
        mn = level(1, [at_, state.get("Mfree2")])
        yield
        b = xbank()
        for n in range(4):
            m = pe.matmul(bk(b)[:, n, :], k[:, ch[n]], q[:, ch[n]], start=True, stop=True, after=[norm, free[b] if n == 0 else None])
        qk = ve.tensor_tensor(qkT[:, p], bk(b), Dm[:], ALU.mult, after=[m, E, state.get(("rec", p))])
        free[b] = qk
        state["Dfree"] = qk
        yield
        b = xbank()
        for n in range(4):
            m = pe.transpose(bk(b)[:, n, :], k[:, ch[n]], ident, after=[norm[1], l_ident, free[b] if n == 0 else None])
        kgo = ve.tensor_tensor(kg[:], bk(b), bc(egn[:, col]), ALU.mult, after=[m, gt["egn"], state.get("kgfree")])
        kdo = ve.tensor_tensor(kd[:, p], bk(b), bc(ekd[:, col]), ALU.mult, after=[m, gt["ekd"], state.get(("rec", p))])
        free[b] = [kgo, kdo]
        Up = U[:, p]
        u = ve.tensor_tensor(Up, ident.unsqueeze(1).to_broadcast([128, 4, 128]), Mm[:, 0],
                                         ALU.subtract, after=[mk, l_ident, state.get(("rec", p))])
        state[("kdo", h)] = kdo
        yield
        vts = []
        for j in range(2):
            b = xbank()
            v = qkv[:, p, 2 + j, :]
            for n in range(4):
                m = pe.transpose(bk(b)[:, n, :], v[:, ch[n]], ident, after=[silus[2 + j], free[b] if n == 0 else None])
            c = ac.activation(vt[:, p, :, j * 128:(j + 1) * 128], bk(b), ACT.Copy, after=[m, state.get(("rec", p))])
            free[b] = c
            vts.append(c)
            yield
        qkv_free[p] = [qdn, m]
        b = xbank()
        for n in range(4):
            m = pe.transpose(bk(b)[:, n, :], Up[:, n, :], ident, after=[u, free[b] if n == 0 else None])
        t = ac.activation(Tm[:], bk(b), ACT.Copy, after=[m, state.get("Tfree")])
        free[b] = t
        yield
        u0 = u
        for i in range(1, 7):
            b = xbank()
            s = Mm[:, i % 2]
            for n in range(4):
                m = pe.matmul(bk(b)[:, n, :], s[:, n, :], Tm[:, n, :], start=True, stop=True,
                              after=[t, mn, free[b] if n == 0 else None])
            state["Tfree"] = m
            pc = ac.activation(Pm[:], bk(b), ACT.Copy, after=[m, state.get("Pfree")])
            free[b] = pc
            if i < 6:
                mn = level(i + 1, [u0 if i == 1 else prev])
                if i == 5:
                    state["ATfree"] = mn
            else:
                state["Mfree2"] = m
            prev = m
            if i == 6:
                state["Mfree1"] = m
            yield
            mt = None
            if i < 6:
                b = xbank()
                for n in range(4):
                    mt = pe.matmul(bk(b)[:, n, :], Up[:, n, :], Pm[:, n, :], start=True, stop=True,
                                   after=[pc, u, free[b] if n == 0 else None])
                t = ve.tensor_tensor(Tm[:], Tm[:], bk(b), ALU.subtract, after=[mt, t])
                free[b] = t
            b = xbank()
            for n in range(4):
                m = pe.matmul(bk(b)[:, n, :], Pm[:, n, :], Up[:, n, :], start=True, stop=True,
                              after=[pc, u, free[b] if n == 0 else None])
            state["Pfree"] = m
            u = ve.tensor_tensor(Up, Up, bk(b), ALU.subtract, after=[m, u])
            free[b] = u
            yield
        b = xbank()
        for n in range(4):
            m = pe.matmul(bk(b)[:, n, :], kg[:, n, :], Up[:, n, :], start=True, stop=True, after=[u, kgo, free[b] if n == 0 else None])
        state["kgfree"] = m
        w = ac.activation(wT[:, p], bk(b), ACT.Copy, after=[m, state.get(("rec", p))])
        free[b] = w
        state[("rdy", h)] = [u, w, qk, kdo, qdn] + vts
        yield

    def recur(h):
        p = h % 2
        rdy = state[("rdy", h)]
        s = None
        for n in range(4):
            Sn, So = S[:, (n + 1) % 2], S[:, n % 2]
            ts = slice(n * 128, (n + 1) * 128)
            m = pe.matmul(banks[4][:, 0:256], U[:, p, n, :], vt[:, p, n, :], start=True, stop=(n == 0), after=[rdy, free[4]])
            if n:
                m = pe.matmul(banks[4][:, 0:256], wT[:, p, n, :], So, start=False, stop=True, after=[s])
            rn = rr[:, n % 2]
            r = ac.activation(rn, banks[4][:, 0:256], ACT.Copy, after=[m, state.get(("rr", n % 2))])
            free[4] = r
            yield
            if n < 3:
                m = pe.matmul(banks[5][:, 0:256], kd[:, p, n, :], rn, start=True, stop=True, after=[r, free[5]])
                if n == 0:
                    s2_ = ve.tensor_copy(Sn, banks[5][:, 0:256], after=[m, state.get("Sfree")])
                else:
                    s2_ = ve.scalar_tensor_tensor(
                        out=Sn, in0=So, scalar=egl[:, 4 * h + n:4 * h + n + 1], in1=banks[5][:, 0:256],
                        op0=ALU.mult, op1=ALU.add, after=[m, gt["egl"], state.get("Sfree"), s])
                free[5] = s2_
            for j in range(2):
                o_ = banks[6 + j][:, ts]
                dj = slice(j * 128, (j + 1) * 128)
                if n:
                    pe.matmul(o_, So[:, dj], qd[:, p, ts], start=True, stop=False, after=[s, free[6 + j]])
                m = pe.matmul(o_, rn[:, dj], qkT[:, p, n, :], start=(n == 0), stop=True, after=[r, free[6 + j] if n == 0 else None])
            state[("rr", n % 2)] = m
            state["Sfree"] = m
            s = s2_
            yield
        state[("rec", p)] = m
        qf[p] = m
        sq, tt = [], []
        for j in range(2):
            sq.append(ac.activation(osq[:, j, :], banks[6 + j][:], ACT.Square, after=[m, state.get(("sqh", j))]))
        yield
        for j in range(2):
            mo = pe.matmul(banks[5][:], ones, osq[:, j, :], start=(j == 0), stop=(j == 1), after=[sq[j], free[5]])
        state[("sqh", 1)] = mo
        zs = []
        for j in range(2):
            z = zb[:, j, :]
            zs.append(ac.activation(z, z, ACT.Silu, after=[state[("z", h)][j]]))
        tables()
        for j in range(2):
            x = ve.scalar_tensor_tensor(out=ot[:, j, :], in0=banks[6 + j][:],
                                                         scalar=gain("a_o_gain", j), in1=zb[:, j, :],
                                                         op0=ALU.mult, op1=ALU.mult, after=[sq[j], zs[j], l_gain["a_o_gain"], state.get(("ot", j))])
            free[6 + j] = [sq[j], x]
            z_free[j] = x
            tt.append(x)
        l = ac.activation(osq[:, 0, :], banks[5][:], ACT.Ln, bias=const(C_EPS), scale=1.0 / 256, after=[mo])
        free[5] = l
        l = ac.activation(osq[:, 0, :], osq[:, 0, :], ACT.Exp, scale=-0.5, after=[l])
        for j in range(2):
            w = ve.tensor_tensor(OF[2 * h + j], ot[:, j, :], osq[:, 0, :], ALU.mult, after=[l, tt[j], xin_free])
            state[("ot", j)] = w
            of_done[2 * h + j] = w
        state[("sqh", 0)] = w
        yield

    xin_free = [x for _, _, r in XA for x in r] + [acc]

    OH = [(XR[:, i, :], XR[:, 16 + i, :]) for i in range(16)]
    XO = [None] * 16

    def split_o(lo, hi):
        for i in range(lo, hi):
            XO[i] = (*OH[i], split_tile(OF[i], *OH[i], of_done[i], used[-1]))
            yield

    fill = {1: 0.95, HEADS: 0.7, HEADS + 1: 4}
    for i in range(HEADS + 2):
        if i:
            use_banks(NARROW)
        if i == 0:
            second = gemm_head(1)
            merge(chain(first, take(second, 14)), 4, gates(), later=later)
            continue
        gen = [gemm_z(i - 2)] if i >= 2 else []
        gen += [gemm_head(i) if i > 1 else second] if i < HEADS else []
        gen += [split_o(0, 14)] if i == HEADS + 1 else []
        merge(chain(*gen), fill.get(i, 1.15), prep(i - 1) if 1 <= i <= HEADS else None, spread(recur(i - 2), 2) if i >= 2 else None,
              later=later, lead=0)
    drain(split_o(14, 16))

    if stop == "A":
        dumps = [dump(Q, f"OF{i}", OF[i], of_done[i]) for i in range(16)]
        return finish(Q, ctx, loaded[-4:] + dumps)

    sqt = new([2, 512]); sqa = new([512]); rb = new([512]); rt = new([512])
    LOC = top[0]
    a_done = [of_done[15], used[-1], x_last(Q, "scalar"), x_last(Q, "tensor"), x_last(Q, "gpsimd")]
    ldh = [Q.dma("gpsimd", f"xr{k}", H[:, k, :], d["x"][k], a_done) for k in range(8)]
    norm = {}

    def stats(n, tile, dep):
        s = ac.activation(sqt[:, n % 2, :], tile, ACT.Square, after=[dep, norm.get(n % 2)])
        if n == 7:
            norm["last"] = s
            return s
        if n == 0:
            a = ve.tensor_copy(sqa[:], sqt[:, 0, :], after=[s, norm.get("acc")])
        else:
            a = ve.tensor_tensor(sqa[:], sqa[:], sqt[:, n % 2, :], ALU.add, after=[s, norm["acc"]])
        norm[n % 2] = norm["acc"] = a
        return a

    def rstd():
        pe.matmul(banks[2][:], ones, sqa[:], start=True, stop=False, after=[norm["acc"], l_ones, free[2]])
        m = pe.matmul(banks[2][:], ones, sqt[:, 1, :], start=False, stop=True, after=[norm["last"]])
        norm[1] = m
        a = ac.activation(rt[:], banks[2][:], ACT.Ln, bias=const(C_EPS), scale=1.0 / 1024, after=[m, l_cc])
        free[2] = a
        norm["acc"] = m
        return ac.activation(rb[:], rt[:], ACT.Exp, scale=-0.5, after=[a, norm.get("rb")])

    def scaled_split(key, dst, ready, *deps, more=True):
        X = []
        for k in range(8):
            xh, xl = dst[k]
            g = gain(key, k)
            hi = ac.activation(xh, H[:, k, :], ACT.Copy, scale=g, after=[ready[k], l_gain[key], deps])
            lo = ve.scalar_tensor_tensor(out=xl, in0=H[:, k, :], scalar=g, in1=xh.bitcast(F),
                                         op0=ALU.mult, op1=ALU.subtract, after=[hi, ready[k], deps])
            X.append((xh, xl, [hi, lo]))
            if k == 1 and more:
                ahead(4)
        return X

    h_ready = [None] * 8

    def evac_h(dep):
        def f(n, bank, last):
            h_ready[n] = ve.tensor_tensor(H[:, n, :], bank[:], H[:, n, :], ALU.add, after=[last, dep[n]])
            stats(n, H[:, n, :], h_ready[n])
            return h_ready[n]
        return f

    norm["acc"] = norm[0] = norm[1] = a_done
    use_banks(WIDE)
    drain(gemm([[("wao", 2 * n), ("wao", 2 * n + 1)] for n in range(8)], XO, evac_h(ldh)))
    if stop == "x1":
        dumps = [dump(Q, f"H{i}", H[:, i, :], h_ready[i]) for i in range(8)]
        return finish(Q, ctx, loaded[-4:] + dumps)

    def slot(i):
        return XR[:, i, :]

    B = Area(LOC, END)
    kpad = B.new([4, 2, 512]); vz = B.new([4, 9, 64])
    qb = B.new([3, 512]); bias = B.new([2, 2, 256]); L = B.new([2, 2, 4, 256]); pT = B.new([4, 4, 128])
    sinks = B.new([32]); mx = B.new([2, 8]); nmx = B.new([2, 8]); den = B.new([2, 8]); es = B.new([2, 8])
    rel = B.new([32]); flip = B.new([128]); hot = L[:, 0].rearrange("p a b c -> p (a b c)")[:, 0:384]
    neg = L[:, 0].rearrange("p a b c -> p (a b c)")[:, 512:896]
    tab = L[:, 0].rearrange("p a b c -> p (a b c)")[:, 1024:1408]
    kst = L[:, 1].rearrange("p a b c -> p (a b c)")[:, 0:1024].rearrange("p (a b) -> p a b", a=2)
    scratch = nc.dram_tensor("rel_rows", [32 * 384], F, kind="Internal").ap()
    w_done = used[-1]
    l_flip = Q.dma("gpsimd", "flip", flip[:], d["k_flip"], a_done)
    l_rel = Q.dma("gpsimd", "rel", rel[0:32, :], d["rel"], a_done)
    l_hot = Q.dma("gpsimd", "hot", hot[0:32, :], d["k_hot"], a_done)
    l_neg = Q.dma("gpsimd", "neg", neg[0:32, :], d["k_neg"], a_done)
    l_snk = Q.dma("gpsimd", "snk", sinks[:], d["sinks"], a_done)
    z1 = po.memset(kpad[:], 0.0, after=a_done)
    z2 = po.memset(vz[:], 0.0, after=a_done)

    m = pe.matmul(banks[3][0:32, 0:384], rel[0:32, :], hot[0:32, :], start=True, stop=True,
                  after=[l_rel, l_hot, free[3]])
    t = ve.tensor_tensor(tab[0:32, :], banks[3][0:32, 0:384], neg[0:32, :], ALU.add, after=[m, l_neg, a_done])
    free[3] = t
    tab_out = Q.dma("scalar", "tabo", scratch.rearrange("(h j) -> h j", h=32), tab[0:32, :], t)

    XKV = scaled_split("kv_norm", [(slot(16 + k), slot(24 + k)) for k in range(8)], h_ready, w_done)
    r1 = rstd()
    vtiles = []

    def head_rms(x, ops, n, tmp, sq, key, dep):
        s = ac.activation(sq, x, ACT.Square, after=[ops, dep])
        b = xbank()
        m = pe.matmul(banks[b][:], blk1, sq, start=True, stop=True, after=[s, l_blk1, free[b]])
        a = ac.activation(tmp, banks[b][:], ACT.Ln, bias=const(C_EPS), scale=1.0 / 64, after=[m, dep])
        free[b] = a
        a = ac.activation(tmp, tmp, ACT.Exp, scale=-0.5, bias=const(n), after=[a])
        return ve.scalar_tensor_tensor(out=x, in0=x, scalar=gain(key, 0), in1=tmp, op0=ALU.mult, op1=ALU.mult,
                                       after=[a, l_gain[key]])

    kq = {}

    def evac_kv(n, bank, last):
        if n < 2:
            dst = kst[:, n, :]
        else:
            dst = qb[:, n - 2, :]
        e1 = ve.tensor_tensor(dst, bank[:], rb[:], ALU.mult, after=[last, r1, a_done])
        kq[n] = e1
        return e1

    kn = {}
    copies = {}

    def kv_post():
        for n in range(2):
            b = xbank()
            for c in range(4):
                m = pe.transpose(bk(b)[:, c, :], qb[:, n, c * 128:(c + 1) * 128], ident,
                                 after=[kq[2 + n], l_ident, free[b]])
            for hh in range(2):
                g = 2 * n + hh
                t = ac.activation(vz[:, :, 2 * g + 1, :], bk(b)[:, :, 64 * hh:64 * hh + 64], ACT.Copy, after=[m, z2])
                vtiles.append(t)
            free[b] = t
            qfree[n] = m
            yield
        for n in range(2):
            sq = pT[:].rearrange("p a b c -> p (a b c)")[:, 512 * n:512 * n + 512]
            tm = pT[:].rearrange("p a b c -> p (a b c)")[:, 1024 + 512 * n:1536 + 512 * n]
            kn[n] = head_rms(kst[:, n, :], kq[n], C_ZERO, tm, sq, "k_gain", a_done)
            for hh in range(2):
                g = 2 * n + hh
                src = kst[64 * hh:64 * hh + 64, n, :]
                copies[g] = [Q.dma("sync", f"kp{g}{e}", kpad[64 * e:64 * e + 64, g, e, :], src, kn[n], z1)
                             for e in range(2)]
            yield

    kv_ = gemm([[("wkv", n)] for n in range(4)], XKV, evac_kv, wide=3)
    for _ in range(24):
        next(kv_)
    XB = scaled_split("b_norm", [(slot(k), slot(8 + k)) for k in range(8)], h_ready, w_done, more=False)
    drain(kv_)
    use_banks(NARROW)
    kv_mm = used[-1]
    att = {}
    qfree = [None] * 3
    ready_q, bfree, ofree = {}, [None, None], {}
    OB = [XF[:, 16 + i, :] for i in range(16)]
    z_done = {}

    def falling(v):
        return bass.AP(v.tensor, v.offset + 127, [list(v.ap[0]), [128, 4], [-1, 128]])

    def gemm_qz(j):
        def ev(n, bank, last):
            if n == 0:
                x = qb[:, j % 3, :]
                e1 = ve.tensor_tensor(falling(x), bank[:].rearrange("p (n c) -> p n c", n=4),
                                      rb[:].rearrange("p (n c) -> p n c", n=4), ALU.mult,
                                      after=[last, qfree[j % 3]])
                ready_q[j] = e1
            else:
                e1 = ve.tensor_tensor(OB[j], bank[:], rb[:], ALU.mult, after=[last, kv_mm])
                z_done[j] = e1
            return e1
        yield from gemm([[("wb", j)], [("wb", 16 + j)]], XB, ev)


    def load_bias(j):
        src = bass.AP(scratch.tensor, 2 * j * 384, [[1, 128], [384, 2], [1, 256]])
        return Q.dma("sync", bsem[j % 2], bias[:, j % 2], src, tab_out, bfree[j % 2])

    bsem = [sem("bias0"), sem("bias1")]
    l_bias = {0: load_bias(0), 1: load_bias(1)}
    qn = {}

    def qnorm(j):
        r = L[:, j % 2].rearrange("p a b c -> p (a b c)")
        qn[j] = head_rms(qb[:, j % 3, :], ready_q[j], C_QB, r[:, 0:512], r[:, 512:1024], "b_q_gain",
                         [att.get(("L", j % 2)), tab_out])

    pend, zs = {}, {}

    def attend(j):
        g, c = j // 4, j % 2
        qn_ = qn[j]
        x = qb[:, j % 3, :]
        Lj = L[:, c]
        mo = []
        for n in range(4):
            b = 4 + n % 2
            lo = 0 if n else 128
            w = 256 - lo
            bb = banks[b][:].rearrange("p (e s) -> p e s", e=2)
            m = pe.matmul(bb[:, :, lo:], x[:, n * 128:(n + 1) * 128],
                          kpad[:, g, :, n * 128 - 128 + lo:n * 128 + 128], start=True, stop=True,
                          after=[qn_, copies[g], free[b]])
            for e in range(2):
                u = 2 * n + e
                o = ve.tensor_tensor_reduce(out=Lj[:, e, n, lo:], in0=bb[:, e, lo:], in1=bias[:, c, e, lo:],
                                            scalar=sinks[:, 2 * j + e:2 * j + e + 1], op0=ALU.add, op1=ALU.max,
                                            accum_out=mx[:, c, u:u + 1],
                                            after=[m, l_bias[j], l_snk, att.get(("L", c)), att.get(("mx", c)), qn_])
            free[b] = o
            mo.append(o)
            yield
        qfree[j % 3] = m
        bfree[c] = o
        if j + 2 < 16:
            l_bias[j + 2] = load_bias(j + 2)
        nm = ve.tensor_scalar(nmx[:, c], mx[:, c], -1.0, None, ALU.mult, after=[mo])
        sk = ve.tensor_tensor(es[:, c].rearrange("p (n e) -> p n e", e=2), nmx[:, c].rearrange("p (n e) -> p n e", e=2),
                              sinks[:, 2 * j:2 * j + 2].unsqueeze(1).to_broadcast([128, 4, 2]), ALU.add,
                              after=[nm, l_snk])
        ps = {}
        pend[j] = ps
        ex = []
        for n in range(4):
            lo = 0 if n else 128
            for e in range(2):
                u = 2 * n + e
                ex.append(ac.activation(Lj[:, e, n, lo:], Lj[:, e, n, lo:], ACT.Exp, bias=nmx[:, c, u:u + 1],
                                        accum_out=den[:, c, u:u + 1], after=[nm, att.get(("mx", c))]))
            yield
        ek = ac.activation(es[:, c], es[:, c], ACT.Exp, after=[sk])
        dn = ve.tensor_tensor(den[:, c], den[:, c], es[:, c], ALU.add, after=[ex, ek])
        rc = ve.reciprocal(den[:, c], den[:, c], after=[dn])
        for n in range(4):
            lo = 0 if n else 128
            for e in range(2):
                u = 2 * n + e
                ps[u] = po.tensor_scalar(Lj[:, e, n, lo:], Lj[:, e, n, lo:], den[:, c, u:u + 1], 1.0,
                                         ALU.mult, ALU.mult, after=[rc, ex])
        att[("mx", c)] = ps[7]
        yield

    def attend2(j):
        g, c = j // 4, j % 2
        Lj, ps = L[:, c], pend[j]
        if j % 2 == 0:
            for jj in (j, j + 1):
                zs[jj] = ac.activation(OB[jj], OB[jj], ACT.Silu, after=[z_done[jj]])
            tables()
        for n in range(4):
            b = xbank()
            first = True
            for kb in ((0, 1) if n else (1,)):
                for e in range(2):
                    m = pe.transpose(bk(b)[:, 2 * kb + e, :], Lj[:, e, n, kb * 128:(kb + 1) * 128], flip[:],
                                     after=[ps[2 * n + e], l_flip, free[b] if first else None])
                    first = False
            k0 = 0 if n else 2
            if n % 2:
                t = ac.activation(pT[:, n, k0:], bk(b)[:, k0:], ACT.Copy, after=[m, att.get(("pT", n))])
            else:
                t = ve.tensor_copy(pT[:, n, k0:], bk(b)[:, k0:], after=[m, att.get(("pT", n))])
            free[b] = t
            ps[("t", n)] = t
            yield
        att[("L", c)] = m
        b = 6 + j % 2
        for n in range(4):
            kbs = (0, 1) if n else (1,)
            for kb in kbs:
                for e in range(2):
                    vb = n - 1 + kb
                    w = vz[:, vb].rearrange("p a d -> p (a d)")
                    s0 = 64 * (2 * g + 1) - 64 * e
                    m = pe.matmul(bk(b)[:, n, :], w[:, s0:s0 + 128], pT[:, n, 2 * kb + e, :],
                                  start=(kb == kbs[0] and e == 0), stop=(kb == 1 and e == 1),
                                  after=[ps[("t", n)], vtiles, free[b]])
            att[("pT", n)] = m
            yield
        o = ve.tensor_tensor(OB[j], banks[b][:], OB[j], ALU.mult, after=[m, zs[j]])
        free[b] = o
        ofree[j] = o
        yield

    def tiles(j):
        yield from gemm_qz(j)
        qnorm(j)

    XOB = [None] * 16

    def split_ob(lo, hi):
        for i in range(lo, hi):
            XOB[i] = (*OH[i], split_tile(OB[i], *OH[i], ofree[i], used[-1]))
            yield

    merge(gemm_qz(0), 2, kv_post())
    att[("L", 1)] = list(copies.values())
    qnorm(0)
    merge(tiles(1), 2, attend(0), None)
    for j in range(16):
        side = tiles(j + 2) if j < 14 else (split_ob(0, 14) if j == 15 else None)
        merge(side, 0.85, attend2(j), attend(j + 1) if j < 15 else None, lead=4)
    drain(split_ob(14, 16))
    if stop == "B":
        dumps = [dump(Q, f"OF{i}", OB[i], ofree[i]) for i in range(16)]
        return finish(Q, ctx, loaded[-4:] + dumps)
    hr = list(h_ready)
    norm["acc"] = norm[0] = norm[1] = norm["acc"]
    norm["rb"] = x_last(Q, "vector")
    use_banks(WIDE)
    drain(gemm([[("wbo", 2 * n), ("wbo", 2 * n + 1)] for n in range(8)], XOB, evac_h(hr)))
    if stop == "x2":
        dumps = [dump(Q, f"H{i}", H[:, i, :], h_ready[i]) for i in range(8)]
        return finish(Q, ctx, loaded[-4:] + dumps)
    b_done = [x_last(Q, e) for e in ("vector", "scalar", "tensor", "gpsimd")]

    XC = scaled_split("g_mix_pre", [(slot(k), slot(8 + k)) for k in range(8)], h_ready, used[-1])
    r2 = rstd()
    C = Area(LOC, END)
    qt = C.new([2, 512]); kp = C.new([2, 2, 512]); vst = C.new([512]); vc = C.new([2, 4, 3, 64])
    sp = C.new([2, 3, 512]); am = C.new([2, 2, 512]); spsum = C.new([2, 512])
    yt = C.new([2, 512]); ysq = C.new([512]); yrt = C.new([512])
    up = C.new([528]); ua = C.new([528]); ub = C.new([528]); wpool = C.new([4, 128]); smask = C.new([128])
    l_smask = Q.dma("scalar", "smask", smask[:], d["k_smask"], b_done)
    z3 = po.memset(kp[:], 0.0, after=[b_done])
    z4 = po.memset(vc[:], 0.0, after=[b_done])
    z5 = po.memset(up[:, 0:16], 0.0, after=[b_done])
    z6 = po.memset(ua[:, 0:16], 0.0, after=[b_done])
    z7 = po.memset(ub[:, 0:16], 0.0, after=[b_done])
    l_wp = Q.dma("scalar", "wpool", wpool[:], d["wpool"], b_done)
    Y = [(slot(16 + i), slot(24 + i)) for i in range(8)]
    XY = [None] * 8
    cs = {}
    pooled = []

    def gemm_qkv(j):
        p = j % 2

        def ev(n, bank, last):
            if n == 0:
                x = ve.scalar_tensor_tensor(out=qt[:, p], in0=bank[:], scalar=0.125, in1=rb[:], op0=ALU.mult,
                                            op1=ALU.mult, after=[last, r2, b_done, cs.get(("q", p))])
                cs[("lq", j)] = x
            elif n == 1:
                xs = [ve.tensor_tensor(kp[64 * e:64 * e + 64, p, e, :], bank[64 * e:64 * e + 64, :],
                                       rb[64 * e:64 * e + 64, :], ALU.mult,
                                       after=[last, r2, z3, cs.get(("q", p))]) for e in range(2)]
                cs[("lk", j)] = xs
                x = xs[1]
            else:
                x = ve.tensor_tensor(vst[:], bank[:], rb[:], ALU.mult, after=[last, r2, b_done, cs.get("vst")])
                def turned():
                    b = 6 + p
                    for c in range(4):
                        m = pe.transpose(bk(b)[:, c, :], vst[:, c * 128:(c + 1) * 128], ident,
                                         after=[x, l_ident, free[b]])
                    cs["vst"] = m
                    o = vc[:, p, :, 0:3:2, :]
                    t = ac.activation(o, bk(b).rearrange("p c (e d) -> p c e d", e=2), ACT.Copy,
                                      after=[m, z4, cs.get(("q", p))])
                    free[b] = t
                    cs[("lv", j)] = t

                if j:
                    turned()
                else:
                    pooled.append(turned)
            return x

        yield from gemm([[("wc", j)], [("wc", 4 + j)], [("wc", 8 + j)]], XC, ev, wide=0 if j else 3)

    def stick(j, e, last_of_pair):
        p = j % 2
        po_b = 6 + p
        pb = banks[po_b]
        zb, ms, xs = {}, {}, {}
        c = e

        def view(i):
            return banks[zb[i]][:, 0:512 - 128 * i]

        def logits(i):
            t0, w = 128 * i, 512 - 128 * i
            b = zb[i] = 2 + 2 * e + i % 2
            z, s_ = view(i), sp[:, c, i % 3, 0:w]
            pe.matmul(z, kp[:, p, e, t0:t0 + 128], qt[:, p, t0:], start=True, stop=False,
                      after=[cs[("lq", j)], cs[("lk", j)], free[b]])
            m = pe.matmul(z[:, 0:128], ident, smask[:], start=False, stop=True, after=[l_ident, l_smask])
            a = ac.activation(s_, z, ACT.Abs, after=[m, cs.get(("sp", c, i % 3)), b_done])
            a = ac.activation(s_, s_, ACT.Exp, scale=-1.0, after=[a])
            a = ac.activation(s_, s_, ACT.Ln, bias=const(C_ONE), after=[a])
            ms[i] = ve.scalar_tensor_tensor(out=s_, in0=z, scalar=0.0, in1=s_, op0=ALU.max, op1=ALU.add,
                                            after=[a])

        def weights(i):
            t0, w = 128 * i, 512 - 128 * i
            z, s_, a_ = view(i), sp[:, c, i % 3, 0:w], am[:, c, i % 2, 0:w]
            if i < 3:
                pe.matmul(z[:, 128:], nones, spsum[:, c, t0 + 128:], start=False, stop=False,
                          after=[cs[("sum", c)], ms[i], l_nones])
            m = pe.matmul(z, ntri, s_, start=False, stop=True, after=[ms[i], l_ntri])
            if i == 3:
                cs[("sum", c)] = ve.tensor_copy(spsum[:, c, t0:], s_, after=[ms[i], cs.get(("sumf", c)), b_done])
            elif i:
                u1 = ve.tensor_tensor(spsum[:, c, t0 + 128:], spsum[:, c, t0 + 128:], s_[:, 128:], ALU.add,
                                      after=[m, cs[("sum", c)]])
                u2 = ve.tensor_copy(spsum[:, c, t0:t0 + 128], s_[:, 0:128], after=[ms[i], cs.get(("sumf", c))])
                cs[("sum", c)] = [u1, u2]
            else:
                cs[("sumf", c)] = m
            cs[("sp", c, i % 3)] = [m, cs[("sum", c)]]
            xs[i] = ac.activation(a_, z, ACT.Exp, after=[m, cs.get(("am", c, i % 2)), b_done])
            free[zb[i]] = xs[i]

        def values(i):
            t0, w = 128 * i, 512 - 128 * i
            wv = vc[:, p, i].rearrange("p a d -> p (a d)")[:, 64 * e:64 * e + 128]
            first = cs.get(("first", j)) is None
            cs[("first", j)] = 1
            m = pe.matmul(pb[:, t0:], wv, am[:, c, i % 2, 0:w], start=first, stop=(last_of_pair and i == 0),
                          after=[xs[i], cs[("lv", j)], free[po_b] if first else None])
            cs[("am", c, i % 2)] = m
            return m

        logits(3)
        yield
        logits(2)
        yield
        weights(3)
        yield
        logits(1)
        yield
        weights(2)
        yield
        values(3)
        yield
        logits(0)
        yield
        weights(1)
        yield
        values(2)
        yield
        weights(0)
        yield
        values(1)
        yield
        m = values(0)
        yield
        if cs.setdefault(("done", j), 0) == 0:
            cs[("done", j)] = 1
            return
        s = ac.activation(ysq[:], pb[:], ACT.Square, after=[m, cs.get("ysq"), b_done])
        yield
        b = 2
        mm = pe.matmul(banks[b][:], blk1, ysq[:], start=True, stop=True, after=[s, l_blk1, free[b]])
        cs["ysq"] = mm
        a = ac.activation(yrt[:], banks[b][:], ACT.Ln, bias=const(C_EPS), scale=1.0 / 64, after=[mm, cs.get("yrt"), b_done])
        free[b] = a
        a = ac.activation(yrt[:], yrt[:], ACT.Exp, scale=-0.5, after=[a])
        y = ve.scalar_tensor_tensor(out=yt[:, p], in0=pb[:], scalar=gain("g_sb", j), in1=yrt[:], op0=ALU.mult,
                                    op1=ALU.mult, after=[a, s, l_gain["g_sb"], cs.get(("yt", p)), b_done])
        cs["yrt"] = y
        free[po_b] = y
        cs[("q", p)] = [m, y]
        XY[4 + j] = (*Y[4 + j], split_tile(yt[:, p], *Y[4 + j], y, used_bo))
        cs[("yt", p)] = XY[4 + j][2]
        yield

    used_bo = used[-1]

    def two(j):
        a, b = stick(j, 0, False), stick(j, 1, True)
        live = [a, b]
        while live:
            for g in list(live):
                if next(g, g) is g:
                    live.remove(g)
            yield

    def pool(j, bank, last):
        x = ve.tensor_tensor(up[:, 16:], bank[:], rb[:], ALU.mult, after=[last, r2, z5, cs.get("up")])
        src, t = up, x
        for k in range(j + 1):
            dst = ua if k % 2 == 0 else ub
            t = ve.tensor_tensor(dst[:, 16:], src[:, 16:], src[:, 16 - (1 << k):528 - (1 << k)], ALU.add,
                                 after=[t, z6, z7, cs.get("uab")])
            src = dst
        c = ve.tensor_tensor(src[:, 16:32], src[:, 16:32], corr[:, j, :], ALU.mult, after=[t, l_corr])
        dd = ub if src is ua else ua
        t = ve.scalar_tensor_tensor(out=dd[:, 16:], in0=src[:, 16:], scalar=0.5 ** (j + 1), in1=up[:, 16:],
                                    op0=ALU.mult, op1=ALU.subtract, after=[c, t])
        cs["up"] = t

        def rest():
            b = 7 - (cs["pair"] % 2)
            m = pe.matmul(banks[b][:], wpool[:, j, :], dd[:, 16:], start=True, stop=True, after=[t, l_wp, free[b]])
            cs["uab"] = m
            y = ac.activation(yt[:, j % 2], banks[b][:], ACT.Copy, scale=gain("pool_scale", j),
                              after=[m, l_gain["pool_scale"], cs.get(("yt", j % 2)), b_done])
            free[b] = y
            XY[j] = (*Y[j], split_tile(yt[:, j % 2], *Y[j], y, used_bo))
            cs[("yt", j % 2)] = XY[j][2]

        pooled.append(rest)
        return x

    def with_rest(g):
        for step, _ in enumerate(g):
            while step == 6 and pooled:
                pooled.pop(0)()
            yield

    def gemm_u(*js):
        for j in js:
            yield from with_rest(gemm([[("wc", 12 + j)]], XC, lambda n, bank, last: pool(j, bank, last)))

    cs["pair"] = 0
    drain(gemm_qkv(0))
    drain(gemm_u(3))
    use_banks(NARROW)
    for j in range(3):
        cs["pair"] = j
        merge(chain(gemm_u(2 - j), with_rest(gemm_qkv(j + 1))), (1.9, 1.9, 2.1)[j], two(j), lead=3)

    D = Area(LOC, END)
    xm = D.new([16, 512], R, "xm"); mo = D.new([8, 512])
    pf = D.new([2, 512]); xp = D.new([4, 512], R, "xp")
    XM = [(xm[:, k, :], xm[:, 8 + k, :]) for k in range(8)]

    def evac_mo(n, bank, last):
        s = stats(n, bank[:], last)
        cs[("mo", n)] = ac.activation(mo[:, n, :], bank[:], ACT.Copy, after=[last, cs["c_done"], cs.get("mo")])
        return [s, cs[("mo", n)]]

    use_banks([0, 1, 6])
    mix = gemm([[("wco", n)] for n in range(8)], XY, evac_mo, wide=3)
    merge(take(mix, 21), 1.1, two(3), lead=2)
    c_done = cs["c_done"] = [x_last(Q, e) for e in ("vector", "scalar", "tensor", "gpsimd")]
    use_banks([4, 5, 7, 0, 1, 6])

    def post(key, dst, next_gain, *deps, beside=()):
        r = rstd()
        drain(beside)
        acc = norm["acc"]
        X = []
        for n in range(8):
            a = ve.scalar_tensor_tensor(out=mo[:, n, :], in0=mo[:, n, :], scalar=gain(key, n), in1=rb[:],
                                        op0=ALU.mult, op1=ALU.mult, after=[r, cs[("mo", n)], acc, l_gain[key]])
            h = h_ready[n] = (po if n else ve).tensor_tensor(H[:, n, :], H[:, n, :], mo[:, n, :], ALU.add, after=[a, h_ready[n]])
            xh, xl = dst[n]
            g = gain(next_gain, n) if next_gain else 1.0
            hi = ac.activation(xh, H[:, n, :], ACT.Copy, scale=g, after=[h, l_g, deps])
            X.append((xh, xl, h, hi, g))
            if n:
                lower(X, n - 1, deps)
            if n == 1:
                ahead(4)
        lower(X, 7, deps)
        cs["mo"] = norm["rb"] = h_ready[7]
        return X

    def lower(X, n, deps):
        xh, xl, h, hi, g = X[n]
        if type(g) is float:
            lo = ve.tensor_tensor(xl, H[:, n, :], xh.bitcast(F), ALU.subtract, after=[hi, h, deps])
        else:
            lo = ve.scalar_tensor_tensor(out=xl, in0=H[:, n, :], scalar=g, in1=xh.bitcast(F), op0=ALU.mult,
                                         op1=ALU.subtract, after=[hi, h, deps])
        X[n] = (xh, xl, [hi, lo])

    norm["rb"] = c_done
    drain(mix)
    XM_ = post("g_mix_post", XM, "g_mlp_pre", c_done)
    if stop == "h3":
        dumps = [dump(Q, f"H{i}", H[:, i, :], h_ready[i]) for i in range(8)]
        return finish(Q, ctx, loaded[-4:] + dumps)

    hid = [None] * 16
    ft = sqt
    cs["ft0"] = cs["ft1"] = norm["acc"]

    def evac_up(base):
        def f(n, bank, last):
            t = ve.scalar_tensor_tensor(out=ft[:, n % 2, :], in0=bank[:], scalar=0.0, in1=rb[:], op0=ALU.max,
                                        op1=ALU.mult, after=[last, r3, cs[f"ft{n % 2}"], norm[n % 2]])
            a = ac.activation(ft[:, n % 2, :], ft[:, n % 2, :], ACT.Square, after=[t])
            hid[n] = (*OH[n], split_tile(ft[:, n % 2, :], *OH[n], a, base))
            cs[f"ft{n % 2}"] = hid[n][2]
            return t
        return f

    def evac_down0(n, bank, last):
        t = ac.activation(mo[:, n, :], bank[:], ACT.Copy, after=[last, h_ready])
        cs[("mo", n)] = t
        return t

    def evac_down1(n, bank, last):
        t = ve.tensor_tensor(mo[:, n, :], bank[:], mo[:, n, :], ALU.add, after=[last, cs[("mo", n)]])
        cs[("mo", n)] = t
        stats(n, mo[:, n, :], t)
        return t

    up_ = gemm([[("wu", n)] for n in range(16)], XM_, evac_up(used[-1]), wide=3)
    for n in range(8):
        stats(n, H[:, n, :], h_ready[n])
        for _ in range(3 if n < 7 else 0):
            next(up_)
    r3 = rstd()
    for _ in range(3):
        next(up_)
    cs["ft0"] = cs["ft1"] = norm["acc"]
    drain(up_)
    for half in range(2):
        if half:
            drain(gemm([[("wu", 16 + n)] for n in range(16)], XM_, evac_up(used[-1])))
            norm["acc"] = norm[0] = norm[1] = [norm["acc"], cs["ft0"], cs["ft1"]]
            XP = []
            for k in range(2):
                l = Q.dma("gpsimd", f"p{k}", pf[:, k, :], d["p"][k], c_done)
                XP.append((xp[:, k, :], xp[:, 2 + k, :], split_tile(pf[:, k, :], xp[:, k, :], xp[:, 2 + k, :], l,
                                                                    c_done)))
        drain(gemm([[("wd", 16 * half + 2 * n), ("wd", 16 * half + 2 * n + 1)] for n in range(8)], hid,
                   evac_down1 if half else evac_down0))

    d_done = used[-1]
    E_ = [XF[:, k, :] for k in range(8)]
    ee = [None] * 8

    squares, sq_free = [], [None, None]

    def sums(f):
        sq_free[f % 2] = pe.matmul(banks[3][:], ones, pf[:, f % 2, :], start=f == 0, stop=f == 7,
                                   after=[squares[f], free[3] if f == 0 else None])

    def ple():
        for half in range(2):
            i, ah, alo_, ready = block("wp", half)
            ah = wh[:, i % NSPL, :].rearrange("p (n k m) -> p n k m", n=4, k=2)
            alo_ = wl[:, i % NSPL, :].rearrange("p (n k m) -> p n k m", n=4, k=2)
            for n in range(4):
                b = next_bank()
                for k in range(2):
                    last = mm3(banks[b][:], ah[:, n, k, :], alo_[:, n, k, :], XP[k][0], XP[k][1], k == 0, k == 1,
                               ready, XP[k][2], free[b] if k == 0 else None)
                if n == 3:
                    used[i] = last
                f = 4 * half + n
                ee[f] = ac.activation(E_[f], banks[b][:], ACT.Copy, after=[last, d_done])
                s = ac.activation(pf[:, f % 2, :], banks[b][:], ACT.Square,
                                  after=[last, sq_free[f % 2], XP[0][2], XP[1][2]])
                free[b] = [ee[f], s]
                if f:
                    sums(f - 1)
                squares.append(s)
                yield
        sums(7)

    norm["rb"] = [norm["acc"], x_last(Q, "vector")]
    pl = ple()
    for _ in range(4):
        next(pl)
    XG = post("g_mlp_post", XM, None, d_done, beside=pl)
    if stop == "h4":
        dumps = [dump(Q, f"H{i}", H[:, i, :], h_ready[i]) for i in range(8)]
        return finish(Q, ctx, loaded[-4:] + dumps)
    stores = []

    def evac_gate(n, bank, last):
        s = ac.activation(mo[:, n, :], bank[:], ACT.Sigmoid, after=[last, h_ready[n]])
        t = ve.tensor_tensor(mo[:, n, :], mo[:, n, :], E_[n], ALU.mult, after=[s, ee[n]])
        t = ve.tensor_tensor(mo[:, n, :], mo[:, n, :], H[:, n, :], ALU.add, after=[t, h_ready[n]])
        stores.append(Q.dma("sync", f"out{n}", out[n], mo[:, n, :], t))
        return s

    gate = gemm([[("wg", n)] for n in range(8)], XG, evac_gate, wide=3)
    a = ac.activation(rt[:], banks[3][:], ACT.Ln, bias=const(C_EPS), scale=1.0 / 1024, after=[sq_free[1], l_cc])
    r4 = ac.activation(rb[:], rt[:], ACT.Exp, scale=-0.5, after=[a, norm["rb"]])
    for f in range(8):
        ee[f] = ve.scalar_tensor_tensor(out=E_[f], in0=E_[f], scalar=gain("g_ple", f), in1=rb[:],
                                        op0=ALU.mult, op1=ALU.mult, after=[r4, ee[f], l_gain["g_ple"]])
    drain(gate)
    return finish(Q, ctx, stores)
    return finish(Q, ctx, loaded[-4:])


def x_last(q, eng):
    return q.q[eng][-1]


def chain(*gens):
    for g in gens:
        yield from g


def spread(g, every):
    for _ in g:
        for _ in range(every - 1):
            yield "pass"
        yield


def take(g, n):
    for _ in range(n):
        next(g)
        yield


def drain(gen):
    for _ in gen:
        pass


def merge(g, n, *others, later=None, lead=0):
    live = [x for x in others if x is not None]
    credit = 0
    for _ in range(lead if g is not None else 0):
        next(g)
    while g is not None or live:
        for x in list(live) or [None]:
            if x is not None:
                r = next(x, x)
                if r is x:
                    live.remove(x)
                elif r == "pass":
                    continue
            credit += n
            if later:
                later.pop(0)()
            while credit >= 1:
                credit -= 1
                if g is not None and next(g, g) is g:
                    g = None
    while later:
        later.pop(0)()


def finish(Q, ctx, stores=()):
    Q.op("sync", lambda e: e.nop(), *stores)
    Q.count()
    block = ctx.enter_context(Q.nc.Block())
    block.sync(lambda e: Q.emit("sync", e))
    block.gpsimd(lambda e: Q.emit("gpsimd", e))
    block.scalar(lambda e: Q.emit("scalar", e))
    block.vector(lambda e: Q.emit("vector", e))
    block.tensor(lambda e: Q.emit("tensor", e))


_N_BUCKETS, _MAX_DIST = 32, 128


def _bucket(dist):
    import numpy as np

    n = np.maximum(dist, 0)
    exact = _N_BUCKETS // 2
    large = exact + (np.log(np.maximum(n, 1) / exact) / np.log(_MAX_DIST / exact)
                     * (_N_BUCKETS - exact)).astype(np.int64)
    return np.where(n < exact, n, np.minimum(large, _N_BUCKETS - 1)).astype(np.int32)


def constants():
    import numpy as np

    f = np.float32
    i = np.arange(128)
    c = {}
    square = [np.eye(128), i[:, None] <= i[None, :], np.ones((128, 128)), i[:, None] // 64 == i[None, :] // 64,
              -1.0 * (i[:, None] >= i[None, :]), -np.ones((128, 128))]
    c["k_flip"] = np.ascontiguousarray(np.eye(128, dtype=f)[::-1])
    c["k_smask"] = np.where(i[:, None] >= i[None, :], -1.0e30, 0.0).astype(f)
    m = np.zeros((128, 7, 128), f)
    for n in range(7):
        b = 1 << n
        m[:, n, :] = ((i[:, None] // (2 * b) == i[None, :] // (2 * b)) & (i[:, None] // b < i[None, :] // b))
    c["k_masks"] = m
    cc = np.zeros((128, 8), f)
    cc[:, 0] = 1e-6
    cc[:, 1] = -0.5 * np.log(128.0)
    cc[:, 2] = -0.5 * np.log(64.0)
    cc[:, 3] = 1.0
    corr = np.ones((128, 4, 16), f)
    for n, w in enumerate((2, 4, 8, 16)):
        corr[:, n, :] = w / np.minimum(np.arange(16) + 1, w)
    c["k_k1"] = np.concatenate([v.astype(f) for v in square] + [cc, corr.reshape(128, 64)], axis=1)
    j = np.arange(384)
    dist = 255 - j
    ok = (dist >= 0) & (dist < 128)
    hot = np.zeros((32, 384), f)
    hot[_bucket(dist), j] = ok
    c["k_hot"] = hot
    c["k_neg"] = np.where(ok, 0.0, -1.0e30).astype(f)[None].repeat(32, 0)
    return c


def layout(i):
    import numpy as np

    a = {k: np.asarray(v) for k, v in i.items()}

    def blocks(w):
        k, n = w.shape
        return np.ascontiguousarray(w.reshape(k // 1024, 8, 128, n // 128, 128).transpose(3, 0, 2, 1, 4)
                                    .reshape(-1, 128, 1024))

    def col(v):
        return np.ascontiguousarray(v.reshape(-1, 128).T)

    w = a["a_w_in"][0]
    tiles = []
    for h in range(8):
        tiles += [w[:, h * 128:h * 128 + 128], w[:, 1024 + h * 128:1152 + h * 128],
                  w[:, 2048 + h * 256:2304 + h * 256], w[:, 4096 + h * 256:4352 + h * 256]]
    d = {}
    d["wa"] = blocks(np.concatenate(tiles, axis=1))
    d["wab"] = np.ascontiguousarray(w[:, 6144:6160].reshape(8, 128, 16).transpose(1, 0, 2))
    d["x"] = np.ascontiguousarray(a["x"][0].T.reshape(8, 128, 512))
    al = np.stack([a["a_A_log"][0], a["a_dt_bias"][0]])
    d["alog"] = np.ascontiguousarray(np.broadcast_to(al[None], (128, 2, 8)))
    d["wao"] = blocks(a["a_w_out"][0])
    d["wkv"] = blocks(a["w_kv"])
    d["wb"] = blocks(a["b_w_in"][0])
    d["wbo"] = blocks(a["b_w_out"][0])
    wc = a["w_in_2"][0]
    d["wc"] = blocks(np.concatenate([wc[:, 512:], wc[:, :512]], axis=1))
    wp = a["w_ple_proj_2"][0]
    d["wp"] = np.ascontiguousarray(wp.reshape(2, 128, 2, 4, 128).transpose(2, 1, 3, 0, 4).reshape(2, 128, 1024))
    d["wco"] = blocks(a["w_out_2"][0])
    d["wu"] = blocks(a["w_up_2"][0])
    wd = a["w_down_2"][0]
    d["wd"] = np.concatenate([blocks(wd[:2048]), blocks(wd[2048:])])
    d["wg"] = blocks(a["w_ple_gate_2"][0])
    d["wpool"] = np.ascontiguousarray(a["w_pool_2"][0].transpose(1, 0, 2))
    d["p"] = np.ascontiguousarray(a["p_2"][0, 0].T.reshape(2, 128, 512))
    d["rel"] = a["rel_bias"]
    d["sinks"] = np.ascontiguousarray(np.broadcast_to(a["b_sinks"].reshape(1, 32), (128, 32)))
    cols = {key: col(a[src]) for key, src in (
        ("a_norm", "a_norm"), ("kv_norm", "kv_norm"), ("b_norm", "b_norm"), ("g_mix_pre", "g_mix_pre_2"),
        ("g_mix_post", "g_mix_post_2"), ("g_mlp_pre", "g_mlp_pre_2"), ("g_mlp_post", "g_mlp_post_2"),
        ("g_ple", "g_ple_2"), ("g_sb", "g_sb_2"), ("pool_scale", "pool_scale_2"), ("a_o_gain", "a_o_gain"))}
    for key in ("k_gain", "b_q_gain"):
        v = a[key].reshape(1, 64)
        cols[key] = np.concatenate([v, v], axis=1).reshape(128, 1)
    conv = a["a_conv"][0].reshape(4, 32, 128).transpose(2, 0, 1).reshape(128, 128)
    d["gains"] = np.ascontiguousarray(np.concatenate([cols[key] for key, _ in GAINS] + [conv], axis=1))
    return d


def kernel(**inputs):
    import numpy as _np
    import concourse.bacc as _bacc
    from concourse import mybir as _mybir
    from concourse.bass_utils import run_bass_kernel_spmd as _run

    nc = _bacc.Bacc("TRN2", target_bir_lowering=False, num_devices=1)
    given = {**layout(inputs), **constants()}
    arrays, args = {}, {}
    for name, a in given.items():
        a = _np.ascontiguousarray(a)
        arrays["in_" + name] = a
        args[name] = nc.dram_tensor("in_" + name, a.shape, _mybir.dt.from_np(a.dtype), kind="ExternalInput").ap()
    out = nc.dram_tensor("out_0_dram", (8, 128, 512), _mybir.dt.float32, kind="ExternalOutput").ap()
    program(nc, args, out)
    r = _run(nc, [arrays], core_ids=[0])
    got = r.results[0]["out_0_dram"]
    return _np.ascontiguousarray(got.reshape(1024, 512).T).reshape(1, 512, 1024)
```
